# Optimizing a Trainium2 kernel written in Bass

```python
import math
import jax, jax.numpy as jnp
from jax import lax
import numpy as np

D_MODEL = 1024
BATCH = 1
SEQ = 1024
DEPTH = 1

ATTN_HEADS = 8
ATTN_KV_HEADS = 2
HEAD_DIM = 64
ATTN_WIDTH = ATTN_HEADS * HEAD_DIM
KV_WIDTH = ATTN_KV_HEADS * HEAD_DIM
IDX_HEADS = 8
IDX_DIM = 64
IDX_TOPK_MAX = 256
Q_BLOCK = 128
SSD_HEADS = 8
SSD_HEAD_DIM = 64
SSD_WIDTH = SSD_HEADS * SSD_HEAD_DIM
SSD_GROUPS = 2
SSD_STATE = 128
SSD_CONV = 4
SSD_CHUNK = 128
CONV_DIM = SSD_WIDTH + 2 * SSD_GROUPS * SSD_STATE
MIX_WIDTH = ATTN_WIDTH + SSD_WIDTH
IN_SIZES = (ATTN_WIDTH, KV_WIDTH, KV_WIDTH, IDX_HEADS * IDX_DIM, IDX_DIM, IDX_HEADS, SSD_WIDTH, CONV_DIM, SSD_HEADS)
D_IN_PROJ = ATTN_WIDTH + 2 * KV_WIDTH + IDX_HEADS * IDX_DIM + IDX_DIM + IDX_HEADS + SSD_WIDTH + CONV_DIM + SSD_HEADS
PEER_HEADS = 8
PEER_NKEYS = 128
PEER_NEXPERTS = PEER_NKEYS * PEER_NKEYS
PEER_KEY_DIM = 128
PEER_HALF = PEER_KEY_DIM // 2
PEER_TOPK = 16
PEER_TOKEN_BLOCK = 128
ROPE_THETA = 10000.0
NORM_EPS = 1e-6

kernel_name = 'hybrid_dsa_ssd_peer_block'

def rmsnorm(x, g):
    xf = x.astype(jnp.float32)
    y = xf * lax.rsqrt(jnp.mean(xf * xf, axis=-1, keepdims=True) + NORM_EPS)
    return (y * g.astype(jnp.float32)).astype(x.dtype)

def rope_tables(positions, dim):
    inv_freq = ROPE_THETA ** (-jnp.arange(0, dim, 2, dtype=jnp.float32) / dim)
    ang = positions.astype(jnp.float32)[..., None] * inv_freq
    return jnp.cos(ang)[:, :, None, :], jnp.sin(ang)[:, :, None, :]

def apply_rope(x, cos, sin):
    half = x.shape[-1] // 2
    x1 = x[..., :half].astype(jnp.float32)
    x2 = x[..., half:].astype(jnp.float32)
    out = jnp.concatenate([x1 * cos - x2 * sin, x2 * cos + x1 * sin], axis=-1)
    return out.astype(x.dtype)

def dsa_attention(q, k, v, q_idx, k_idx, w_idx):
    b_, s_ = q.shape[0], q.shape[1]
    topk = min(IDX_TOPK_MAX, s_ // 4)
    n_blk = s_ // Q_BLOCK
    grp = ATTN_HEADS // ATTN_KV_HEADS
    key_pos = jnp.arange(s_)
    w_scaled = w_idx.astype(jnp.float32) * (IDX_HEADS ** -0.5)

    def block(i):
        start = i * Q_BLOCK
        qb = lax.dynamic_slice_in_dim(q, start, Q_BLOCK, axis=1)
        qib = lax.dynamic_slice_in_dim(q_idx, start, Q_BLOCK, axis=1)
        wib = lax.dynamic_slice_in_dim(w_scaled, start, Q_BLOCK, axis=1)
        qpos = start + jnp.arange(Q_BLOCK)
        causal = key_pos[None, :] <= qpos[:, None]
        logits = jnp.einsum('bqhd,bsd->bqhs', qib, k_idx).astype(jnp.float32) * (IDX_DIM ** -0.5)
        score = jnp.einsum('bqh,bqhs->bqs', wib, jax.nn.relu(logits))
        score = jnp.where(causal[None], score, -jnp.inf)
        _, sel = lax.top_k(score, topk)
        valid = sel <= qpos[None, :, None]
        k_sel = jax.vmap(lambda kb, ib: kb[ib])(k, sel)
        v_sel = jax.vmap(lambda vb, ib: vb[ib])(v, sel)
        qg = qb.reshape(b_, Q_BLOCK, ATTN_KV_HEADS, grp, HEAD_DIM)
        s = jnp.einsum('bqhgd,bqkhd->bqhgk', qg, k_sel).astype(jnp.float32) * (HEAD_DIM ** -0.5)
        s = jnp.where(valid[:, :, None, None, :], s, -jnp.inf)
        p = jax.nn.softmax(s, axis=-1).astype(v.dtype)
        o = jnp.einsum('bqhgk,bqkhd->bqhgd', p, v_sel)
        return o.reshape(b_, Q_BLOCK, ATTN_WIDTH)

    out = lax.map(block, jnp.arange(n_blk))
    return out.transpose(1, 0, 2, 3).reshape(b_, s_, ATTN_WIDTH)

def segsum(a):
    t = a.shape[-1]
    ii = jnp.arange(t)[:, None]
    jj = jnp.arange(t)[None, :]
    ar = jnp.broadcast_to(a[..., :, None], a.shape + (t,))
    ar = jnp.where(ii > jj, ar, 0.0)
    cs = jnp.cumsum(ar, axis=-2)
    return jnp.where(ii >= jj, cs, -jnp.inf)

def ssd_mixer(z, xbc, dt_raw, conv_w, conv_b, dt_bias, a_log, d_skip, norm_g):
    b_, s_ = z.shape[0], z.shape[1]
    f32 = jnp.float32
    xbc = lax.conv_general_dilated(xbc, conv_w[:, None, :].astype(xbc.dtype), window_strides=(1,),
                                   padding=[(SSD_CONV - 1, 0)], dimension_numbers=('NWC', 'WIO', 'NWC'),
                                   feature_group_count=CONV_DIM)
    xbc = jax.nn.silu(xbc + conv_b.astype(xbc.dtype))
    xs = xbc[..., :SSD_WIDTH]
    bm = xbc[..., SSD_WIDTH:SSD_WIDTH + SSD_GROUPS * SSD_STATE]
    cm = xbc[..., SSD_WIDTH + SSD_GROUPS * SSD_STATE:]
    dt = jax.nn.softplus(dt_raw.astype(f32) + dt_bias.astype(f32))
    a = -jnp.exp(a_log.astype(f32))
    nc = s_ // SSD_CHUNK
    r = SSD_HEADS // SSD_GROUPS
    x = xs.astype(f32).reshape(b_, nc, SSD_CHUNK, SSD_GROUPS, r, SSD_HEAD_DIM)
    dtc = dt.reshape(b_, nc, SSD_CHUNK, SSD_GROUPS, r)
    xdt = x * dtc[..., None]
    bc = bm.astype(f32).reshape(b_, nc, SSD_CHUNK, SSD_GROUPS, SSD_STATE)
    cc = cm.astype(f32).reshape(b_, nc, SSD_CHUNK, SSD_GROUPS, SSD_STATE)
    adt = (dtc * a.reshape(SSD_GROUPS, r)).transpose(0, 3, 4, 1, 2)
    a_cum = jnp.cumsum(adt, axis=-1)
    lmat = jnp.exp(segsum(adt))
    cb = jnp.einsum('bclgn,bcsgn->bgcls', cc, bc)
    y_diag = jnp.einsum('bgcls,bgrcls,bcsgrp->bclgrp', cb, lmat, xdt)
    decay_states = jnp.exp(a_cum[..., -1:] - a_cum)
    states = jnp.einsum('bclgn,bgrcl,bclgrp->bcgrpn', bc, decay_states, xdt)
    states = jnp.concatenate([jnp.zeros_like(states[:, :1]), states], axis=1)
    chunk_decay = jnp.exp(segsum(jnp.pad(a_cum[..., -1], ((0, 0), (0, 0), (0, 0), (1, 0)))))
    states = jnp.einsum('bgrzc,bcgrpn->bzgrpn', chunk_decay, states)[:, :-1]
    y_off = jnp.einsum('bclgn,bcgrpn,bgrcl->bclgrp', cc, states, jnp.exp(a_cum))
    y = y_diag + y_off + x * d_skip.astype(f32).reshape(SSD_GROUPS, r)[..., None]
    y = y.reshape(b_, s_, SSD_WIDTH)
    y = rmsnorm(y * jax.nn.silu(z.astype(f32)), norm_g)
    return y.astype(z.dtype)

def peer_ffn(h, w_q, sub_keys, u, v):
    b_, s_, d_ = h.shape
    ht = h.reshape((b_ * s_) // PEER_TOKEN_BLOCK, PEER_TOKEN_BLOCK, d_)

    def block(xb):
        q = (xb @ w_q).reshape(PEER_TOKEN_BLOCK, PEER_HEADS, 2, PEER_HALF)
        s = jnp.einsum('thid,hikd->thik', q, sub_keys).astype(jnp.float32)
        sv, si = lax.top_k(s, PEER_TOPK)
        cand = (sv[..., 0, :, None] + sv[..., 1, None, :]).reshape(PEER_TOKEN_BLOCK, PEER_HEADS, PEER_TOPK * PEER_TOPK)
        cidx = (si[..., 0, :, None] * PEER_NKEYS + si[..., 1, None, :]).reshape(PEER_TOKEN_BLOCK, PEER_HEADS, PEER_TOPK * PEER_TOPK)
        fv, fpos = lax.top_k(cand, PEER_TOPK)
        eidx = jnp.take_along_axis(cidx, fpos, axis=-1)
        g = jax.nn.softmax(fv, axis=-1)
        u_sel = jnp.take(u, eidx, axis=0)
        act = jax.nn.gelu(jnp.einsum('thkd,td->thk', u_sel, xb).astype(jnp.float32), approximate=False) * g
        v_sel = jnp.take(v, eidx, axis=0)
        return jnp.einsum('thk,thkd->td', act.astype(v.dtype), v_sel)

    out = lax.map(block, ht)
    return out.reshape(b_, s_, d_)

def setup_inputs(seed: int = 0) -> dict:
    key = jax.random.key(seed)
    ks = jax.random.split(key, 24)
    f32 = jnp.float32

    def nrm(k, shape, s):
        return jax.random.normal(k, shape, f32) * s

    x = nrm(ks[0], (BATCH, SEQ, D_MODEL), 1.0)
    c = nrm(ks[1], (BATCH, D_MODEL), 1.0)
    offs = jax.random.randint(ks[2], (BATCH, 1), 0, 64, dtype=jnp.int32)
    positions = offs + jnp.arange(SEQ, dtype=jnp.int32)[None, :]
    w_ada = nrm(ks[3], (DEPTH, D_MODEL, 6 * D_MODEL), 0.5 * D_MODEL ** -0.5)
    b_ada = nrm(ks[4], (DEPTH, 6 * D_MODEL), 0.02)
    pre_mix_g = 1.0 + nrm(ks[5], (DEPTH, D_MODEL), 0.02)
    post_mix_g = 1.0 + nrm(ks[6], (DEPTH, D_MODEL), 0.02)
    w_in = nrm(ks[7], (DEPTH, D_MODEL, D_IN_PROJ), D_MODEL ** -0.5)
    conv_w = nrm(ks[8], (DEPTH, SSD_CONV, CONV_DIM), SSD_CONV ** -0.5)
    conv_b = nrm(ks[9], (DEPTH, CONV_DIM), 0.02)
    dt0 = jnp.exp(jax.random.uniform(ks[10], (DEPTH, SSD_HEADS), f32, math.log(1e-3), math.log(1e-1)))
    dt_bias = dt0 + jnp.log(-jnp.expm1(-dt0))
    a_log = jnp.log(jax.random.uniform(ks[11], (DEPTH, SSD_HEADS), f32, 1.0, 16.0))
    d_skip = 1.0 + nrm(ks[12], (DEPTH, SSD_HEADS), 0.02)
    ssd_norm_g = 1.0 + nrm(ks[13], (DEPTH, SSD_WIDTH), 0.02)
    w_out = nrm(ks[14], (DEPTH, MIX_WIDTH, D_MODEL), MIX_WIDTH ** -0.5)
    pre_ffn_g = 1.0 + nrm(ks[15], (DEPTH, D_MODEL), 0.02)
    post_ffn_g = 1.0 + nrm(ks[16], (DEPTH, D_MODEL), 0.02)
    peer_w_q = nrm(ks[17], (DEPTH, D_MODEL, PEER_HEADS * PEER_KEY_DIM), D_MODEL ** -0.5)
    peer_sub_keys = nrm(ks[18], (DEPTH, PEER_HEADS, 2, PEER_NKEYS, PEER_HALF), PEER_HALF ** -0.5)
    peer_u = nrm(ks[19], (DEPTH, PEER_NEXPERTS, D_MODEL), D_MODEL ** -0.5)
    peer_v = nrm(ks[20], (DEPTH, PEER_NEXPERTS, D_MODEL), D_MODEL ** -0.5)
    return {'x': x, 'c': c, 'positions': positions, 'w_ada': w_ada, 'b_ada': b_ada,
            'pre_mix_g': pre_mix_g, 'post_mix_g': post_mix_g, 'w_in': w_in, 'conv_w': conv_w,
            'conv_b': conv_b, 'dt_bias': dt_bias, 'a_log': a_log, 'd_skip': d_skip,
            'ssd_norm_g': ssd_norm_g, 'w_out': w_out, 'pre_ffn_g': pre_ffn_g, 'post_ffn_g': post_ffn_g,
            'peer_w_q': peer_w_q, 'peer_sub_keys': peer_sub_keys, 'peer_u': peer_u, 'peer_v': peer_v}

def reference(x, c, positions, w_ada, b_ada, pre_mix_g, post_mix_g, w_in, conv_w, conv_b, dt_bias,
              a_log, d_skip, ssd_norm_g, w_out, pre_ffn_g, post_ffn_g, peer_w_q, peer_sub_keys,
              peer_u, peer_v):
    b_, s_, _ = x.shape
    cos, sin = rope_tables(positions, HEAD_DIM)
    split_at = np.cumsum(IN_SIZES)[:-1].tolist()
    for l in range(DEPTH):
        mod = jax.nn.silu(c) @ w_ada[l] + b_ada[l]
        sh1, sc1, g1, sh2, sc2, g2 = jnp.split(mod[:, None, :], 6, axis=-1)
        h = rmsnorm(x, pre_mix_g[l]) * (1.0 + sc1) + sh1
        proj = h @ w_in[l]
        q, k, v, qi, ki, wi, z, xbc, dt_raw = jnp.split(proj, split_at, axis=-1)
        q = apply_rope(q.reshape(b_, s_, ATTN_HEADS, HEAD_DIM), cos, sin)
        k = apply_rope(k.reshape(b_, s_, ATTN_KV_HEADS, HEAD_DIM), cos, sin)
        v = v.reshape(b_, s_, ATTN_KV_HEADS, HEAD_DIM)
        qi = apply_rope(qi.reshape(b_, s_, IDX_HEADS, IDX_DIM), cos, sin)
        ki = apply_rope(ki[:, :, None, :], cos, sin)[:, :, 0, :]
        attn_out = dsa_attention(q, k, v, qi, ki, wi)
        ssd_out = ssd_mixer(z, xbc, dt_raw, conv_w[l], conv_b[l], dt_bias[l], a_log[l], d_skip[l], ssd_norm_g[l])
        mix = jnp.concatenate([attn_out, ssd_out.astype(attn_out.dtype)], axis=-1) @ w_out[l]
        x = x + g1 * rmsnorm(mix, post_mix_g[l])
        h = rmsnorm(x, pre_ffn_g[l]) * (1.0 + sc2) + sh2
        f = peer_ffn(h, peer_w_q[l], peer_sub_keys[l], peer_u[l], peer_v[l])
        x = x + g2 * rmsnorm(f, post_ffn_g[l])
    return x.astype(positions.dtype if False else x.dtype)


_drawn_inputs = setup_inputs


def setup_inputs(seed=0):
    import zlib

    import numpy as np

    out = dict(_drawn_inputs(seed))
    spreads = {}
    factors = {'d_skip': 3.533, 'post_ffn_g': 8.0}
    for name, (base, spread) in spreads.items():
        noise = np.random.default_rng([zlib.crc32(name.encode()), seed]).standard_normal(out[name].shape)
        drawn = base * np.exp(spread * noise) if base else spread * noise
        out[name] = __import__('jax').numpy.asarray(drawn.astype(out[name].dtype))
    for name, factor in factors.items():
        out[name] = (out[name] * factor).astype(out[name].dtype)
    return out
```

```python
import math
from contextlib import ExitStack

import concourse.bass as bass
from concourse import mybir

ALU = mybir.AluOpType
ACT = mybir.ActivationFunctionType
AX = mybir.AxisListType
F32 = mybir.dt.float32
BF16 = mybir.dt.bfloat16
I32 = mybir.dt.int32
U32 = mybir.dt.uint32

P = 128
D = 1024
KC = D // P
SEQ = 1024
NB = SEQ // P
HD = 64
HEADS = 8
HALF = HD // 2
TOPK = 256
NSTATE = 128
CT = 8
TAPS = 4
EXPERT_KEYS = 128
PK = 16
LISTS = 2 * HEADS
SLOTS = HEADS * PK
THETA = 10000.0
EPS = 1e-6

C_QI = 768
C_KI = 1280
C_Z = 1352
C_XBC = 1864
C_DT = 2888
D_IN = 2896

NEG = -1e30
TAKEN = -3e38
LOW = -2e38

UR = 6
VR = 4
GR = 4
LAG = 18
STAGES = 206
LAST = 124
END = 1 << 30


class Signal:

    def __init__(self, sem, per=1):
        self.sem = sem
        self.per = per

    def at(self, b, k):
        return b * self.per + k

    def wait(self, eng, b, k):
        value = self.at(b, k)
        if not (isinstance(value, int) and value == 0):
            eng.wait_ge(self.sem, value)


class Steps:

    def __init__(self, eng, sem):
        self.eng, self.sem, self.n = eng, sem, 0

    def begin(self):
        self.eng.sem_clear(self.sem)
        self.n = 0

    def __call__(self, ins):
        self.n += 1
        ins.then_inc(self.sem, 1)
        self.eng.wait_ge(self.sem, self.n)


class Weave:

    def __init__(self, gen):
        self.gen = gen
        self.stage = next(gen, END)

    def upto(self, stage):
        while self.stage <= stage:
            self.stage = next(self.gen, END)


def slot_stage(n):
    return (n + 1) * STAGES // LAST


def uses(ring, r):
    return len(range(r, SLOTS, ring))


def hybrid_block(nc, x, c, positions, w_ada, b_ada, pre_mix_g, post_mix_g, w_in, conv_w, conv_b, dt_bias,
                 a_log, d_skip, ssd_norm_g, w_out, pre_ffn_g, post_ffn_g, peer_w_q, peer_sub_keys,
                 peer_u, peer_v, out):
    ctx = ExitStack()
    with ctx:
        def sb(name, cols, dt=F32):
            return ctx.enter_context(nc.sbuf_tensor(name, [P, cols], dt))[:, :]

        def sem(name):
            return ctx.enter_context(nc.semaphore(name))

        def sig(name, per=1):
            return Signal(sem(name), per)

        def grid(ap, a):
            return ap.rearrange("p (a n) -> p a n", a=a)

        def over_last(ap, n):
            return ap.unsqueeze(2).to_broadcast([P, ap.shape[1], n])

        def over_first(ap, n):
            return ap.unsqueeze(1).to_broadcast([P, n, ap.shape[1]])

        ident = sb("ident", P)
        upto = sb("upto", P)
        after = sb("after", P)
        ones = sb("ones", P)
        causal = sb("causal", SEQ + 7 * P, BF16)
        iota_i = sb("iota_i", PK, I32)
        iota16 = sb("iota16", PK)
        inv_freq = sb("inv_freq", HALF)
        pos_i = sb("pos_i", NB, I32)
        pos_f = sb("pos_f", NB)
        eps = sb("eps", 1)
        convw = sb("convw", CT * TAPS)
        convb = sb("convb", CT)
        dtb = sb("dtb", HEADS)
        neg_a = sb("neg_a", HEADS)
        dskip = sb("dskip", HEADS)
        ssdg = sb("ssdg", 512)
        P1 = sb("P1", D)
        A2 = sb("A2", D)
        B2 = sb("B2", D)
        P2 = sb("P2", D)
        KV = sb("KV", 4 * SEQ)
        k0T, k1T, kiT = (KV[:, i * SEQ:(i + 1) * SEQ] for i in range(3))
        vv = grid(KV[:, 3 * SEQ:4 * SEQ], NB)
        keysT = grid(sb("keysT", HEADS * P), HEADS)
        W = sb("W", 16384 + 7168)
        w_in_sb = grid(W[:, 0:KC * D_IN], KC)
        w_out_sb = grid(W[:, 0:8192], KC)
        w_q_sb = grid(W[:, 8192:16384], KC)
        T = W[:, 16384:16384 + 7168]
        ring = sb("ring", (UR + VR) * D)
        u_ring = [ring[:, i * D:(i + 1) * D] for i in range(UR)]
        v_ring = [ring[:, (UR + i) * D:(UR + i + 1) * D] for i in range(VR)]
        diag = [sb(f"diag{i}", P) for i in range(GR)]
        HX = sb("HX", 4 * D)
        h2c, x1c, h2n, x1n = (HX[:, i * D:(i + 1) * D] for i in range(4))
        A1, B1 = h2c, x1c
        mix = sb("mix", D)
        state = sb("state", 512)
        hist = grid(sb("hist", CT * 3), CT)
        rowsum = sb("rowsum", NB)
        rstd = sb("rstd", NB)
        dtwi = sb("dtwi", NB * 16)
        dt_s = sb("dt_s", 64)
        adt = sb("adt", 64)
        eac = sb("eac", 64)
        dec = sb("dec", 64)
        etot = sb("etot", 64)
        wis = sb("wis", 64)
        scT = sb("scT", KC)
        stat = sb("stat", 16)
        negmax = sb("negmax", HEADS)
        psums = sb("psums", HEADS)
        rsums = sb("rsums", HEADS)
        mx8 = sb("mx8", 8)
        idxn = sb("idxn", SLOTS, U32)
        gn = sb("gn", SLOTS)
        idxu = sb("idxu", SLOTS, U32)
        idxv = sb("idxv", SLOTS, U32)
        gc = sb("gc", SLOTS)
        gsum = sb("gsum", HEADS)
        dots = sb("dots", SLOTS)
        gel = sb("gel", SLOTS)
        wgt = sb("wgt", SLOTS)

        ada_buf = [ring[:, i * 3072:(i + 1) * 3072] for i in range(3)]
        b_row = KV[0:1, 0:3072]
        keys_raw = grid(KV[:, 3072:4096], HEADS)
        cosT = ring[:, 9216:9472]
        sinT = ring[:, 9472:9728]
        ang = ring[:, 9728:9984]
        ang2 = ring[:, 9984:10240]
        hT = grid(ring[:, 0:D], KC)
        stag = ring[:, D:D + 2560]
        raw = ring[:, 3584:4992]
        rot = ring[:, 4992:6400]
        rtmp = mix[:, 0:704]
        small = T[:, 4480:4480 + 6 * 64]
        qT = grid(T[:, 0:512], 4)
        qiT = grid(T[:, 512:1024], 4)
        xc = grid(T[:, 1024:1024 + CT * 131], CT)
        L = T[:, 1024:2048]
        cv = grid(T[:, 2072:3096], CT)
        ctmp = grid(T[:, 3096:4120], CT)
        xtok = T[:, 3096:3608]
        btok = T[:, 3608:3864]
        xdt = T[:, 3864:4376]
        xw = T[:, 4376:4888]
        gh = grid(T[:, 4888:5400], 4)
        yy = T[:, 5400:5912]
        ytmp = T[:, 5912:6424]
        cbm = grid(T[:, 6424:6680], 2)
        zt = mix[:, 512:1024]
        SC = T[:, 1024:2048]
        AM = T[:, 2048:3072]
        RL = [T[:, 3072:4096], T[:, 4096:5120]]
        PT = grid(T[:, 5120:6144], NB)
        mixT = grid(T[:, 0:1024], KC)
        otmp = T[:, 1024:2048]
        h2T = grid(T[:, 2048:3072], KC)
        qpT = grid(T[:, 3072:4096], HEADS)
        ss = T[:, 4096:6144]
        cand = T[:, 0:2048]
        hot = T[:, 2048:4096]
        sv = T[:, 6144:6400]
        si = T[:, 6400:6656].bitcast(U32)
        sif = T[:, 6656:6912]
        fv = T[:, 6912:7040]
        fp = T[:, 7040:7168].bitcast(U32)
        fpi = T[:, 4096:4224].bitcast(U32)
        fpf = T[:, 4224:4352]
        e1 = T[:, 4352:4480]

        ps = ctx.enter_context(nc.psum_tensor("ps", [P, 8 * 512], F32))[:, :]

        def bank(i, n=1):
            return ps[:, i * 512:(i + n) * 512]

        VB, SB, TB, OB, XB = bank(0, 2), bank(2, 2), bank(4, 2), bank(6), bank(7)

        spill = nc.dram_tensor("spill", [NB, P, 2560], F32, kind="Internal").ap()

        s_consts = sem("consts_ready")
        s_conststep = sem("const_steps")
        s_small = sem("small_in")
        s_rows = sem("c_positions_in")
        s_gain = sem("gain_in")
        s_brow = [sem("b_ada_in0"), sem("b_ada_in1")]
        s_keys = sem("keys_in")
        s_ada = [sem(f"ada_in{i}") for i in range(3)]
        s_xs = sem("x_stat_in")
        s_sumsq = sem("x_sumsq")
        s_wide = sem("silu_c_wide")
        s_silu = sem("silu_c")
        s_adaused = sem("ada_used")
        s_mod = sem("mod_done")
        s_keyps = sem("keys_psum")
        s_keysT = sem("keys_T")
        s_ang = sem("angles_ready")
        s_trig = sem("trig_ready")
        s_root = sem("x_root")
        s_win = sem("w_in_in")
        s_wout = sem("w_out_in")
        s_wq = sem("w_q_in")

        a_x = sig("a_x_in", 16)
        a_h = sig("a_h")
        a_hps = sig("a_hT_psum")
        a_hT = sig("a_hT")
        a_proj = sig("a_proj", 6)
        a_raw = sig("a_raw")
        a_rope = sig("a_rope")
        a_rps = sig("a_rot_psum")
        a_rot = sig("a_rot")
        a_xbc = sig("a_xbc")
        a_out = sig("a_spilled", 16)
        s_dtv = sem("dt_vector")
        s_dta = sem("dt_scalar")
        s_dtp = sem("dt_psum")

        m_xbc = sig("m_xbc_in", 16)
        m_z = sig("m_z_in", 16)
        m_qq = sig("m_qq_in", 16)
        m_x = sig("m_x_in", 16)
        conv = sig("conv_done")
        convact = sig("conv_silu", CT)
        zgate = sig("z_silu")
        chanT = sig("channels_psum", 2)
        tok = sig("tokens_ready")
        xwr = sig("xw_ready")
        ghr = sig("gh_ready", 2)
        cbps = sig("cb_psum")
        seg = sig("seg_psum", 2)
        decay = sig("decay_ready", 2)
        masked = sig("masked_ready", 2)
        yoff = sig("yoff_psum")
        stps = sig("state_psum")
        ydiag = sig("ydiag_psum")
        stdone = sig("state_done")
        gated = sig("gated")
        ssdrms = sig("ssd_root")
        ssdout = sig("ssd_out")
        logit = sig("index_psum", HEADS)
        relu = sig("index_relu", HEADS)
        scacc = sig("index_summed", HEADS)
        sps = sig("scores_psum", HEADS)
        sread = sig("scores_read", HEADS)
        smax = sig("max_ready", HEADS)
        sexp = sig("probs_ready", HEADS)
        ptps = sig("probsT_psum", HEADS)
        ptc = sig("probsT_ready", HEADS)
        av = sig("av_psum", HEADS)
        mixr = sig("mix_ready")
        mixps = sig("mixT_psum")
        mixTr = sig("mixT_ready")
        outps = sig("out_psum")
        outrms = sig("out_root")
        x1r = sig("x1_ready")
        x1rms = sig("x1_root")
        h2r = sig("h2_ready")
        h2ps = sig("h2T_psum")
        h2Tr = sig("h2T_ready")
        pqps = sig("peer_q_psum")
        pqr = sig("peer_q_ready")
        pss = sig("sub_scores_psum")
        s2 = sig("sub_scores_ready", 2)
        fvr = sig("top_scores_ready")
        gexp = sig("gate_exp")
        prep = sig("experts_chosen")
        idxc = sig("indices_taken", 2)
        dot = sig("dot_done", SLOTS)
        gelu = sig("gelu_done", HEADS)
        wready = sig("weights_ready", HEADS)
        dg = sig("diag_ready", SLOTS)
        vused = sig("v_used", SLOTS)
        frsum = sig("f_sumsq")
        frms = sig("f_root")
        fread = sig("f_read")
        xfin = sig("x_final")
        xcommit = sig("x1_taken")
        xout = sig("x_out", 16)
        u_in = [sem(f"u_in{r}") for r in range(UR)]
        v_in = [sem(f"v_in{r}") for r in range(VR)]
        vstep = sem("vector_steps")
        pstep = sem("vector_expert_steps")
        astep = sem("scalar_steps")
        bstep = sem("vector_setup_steps")
        rstep = sem("vector_projection_steps")

        s_room = sem("room_seen")
        s_turn = sem("turn_seen")

        block = ctx.enter_context(nc.Block())

        @block.sync
        def _(sp):
            x_blocks = x.rearrange("o (b p) d -> b p (o d)", p=P)
            out_blocks = out.rearrange("o (b p) d -> b p (o d)", p=P)
            sp.dma_start(scT, c.rearrange("o (k p) -> p (o k)", p=P), allow_slow_non_contiguous=True).then_inc(s_rows, 16)
            sp.dma_start(pos_i, positions.rearrange("o (b p) -> p (o b)", p=P), allow_slow_non_contiguous=True).then_inc(s_rows, 16)
            sp.dma_start(b_row, b_ada[0:1, 0:3072]).then_inc(s_brow[0], 16)
            for n in range(2 * KC):
                half, k = n // KC, n % KC
                if n >= 3:
                    sp.wait_ge(s_adaused, n - 2)
                sp.dma_start(ada_buf[n % 3], w_ada[0, k * P:(k + 1) * P, half * 3072:(half + 1) * 3072])\
                    .then_inc(s_ada[n % 3], 16)
                if n == 3:
                    for dst, src in ((A1, pre_mix_g), (P1, post_mix_g), (A2, pre_ffn_g), (P2, post_ffn_g)):
                        sp.dma_start(dst, src[0, :].partition_broadcast(P)).then_inc(s_gain, 16)
                    sp.dma_start(ssdg, ssd_norm_g[0, :].partition_broadcast(P)).then_inc(s_gain, 16)
                if n == KC + 2:
                    sp.dma_start(b_row, b_ada[0:1, 3072:6144]).then_inc(s_brow[1], 16)
            for k in range(KC):
                sp.dma_start(w_in_sb[:, k, :], w_in[0, k * P:(k + 1) * P, :]).then_inc(s_win, 16)
            with sp.Fori(0, NB) as b:
                a_rot.wait(sp, b, 1)
                a_xbc.wait(sp, b, 1)
                sp.dma_start(spill[b], stag).then_inc(a_out.sem, 16)
            a_out.wait(sp, NB, 0)
            a_proj.wait(sp, NB, 0)

            def mix_loads(b):
                prep.wait(sp, b, 0)
                sp.dma_start(xc[:, :, 3:131], spill[b, :, 1536:2560].rearrange("p (a n) -> p a n", a=CT))\
                    .then_inc(m_xbc.sem, 16)
                sp.dma_start(zt, spill[b, :, 1024:1536]).then_inc(m_z.sem, 16)
                sp.dma_start(T[:, 0:1024], spill[b, :, 0:1024]).then_inc(m_qq.sem, 16)
                xcommit.wait(sp, b, 0)
                sp.dma_start(x1n, x_blocks[b]).then_inc(m_x.sem, 16)

            def peer_store(b):
                xfin.wait(sp, b, 1)
                sp.dma_start(out_blocks[b], x1c).then_inc(xout.sem, 16)

            mix_loads(0)
            sp.dma_start(w_out_sb, w_out[0].rearrange("(k p) n -> p k n", p=P)).then_inc(s_wout, 16)
            sp.dma_start(w_q_sb, peer_w_q[0].rearrange("(k p) n -> p k n", p=P)).then_inc(s_wq, 16)
            mix_loads(1)
            peer_store(0)
            with sp.Fori(1, NB - 1) as b:
                mix_loads(b + 1)
                peer_store(b)
            peer_store(NB - 1)
            xout.wait(sp, NB, 0)

        @block.gpsimd
        def _(pool):
            n = 0

            def made(ins):
                nonlocal n
                n += 1
                ins.then_inc(s_conststep, 1)
                pool.wait_ge(s_conststep, n)

            made(pool.memset(ident, 0.0))
            made(pool.affine_select(out=ident, in_=ident, compare_op=ALU.not_equal, fill=1.0, base=0,
                                    pattern=[[-1, P]], channel_multiplier=1))
            made(pool.memset(ones, 1.0))
            made(pool.affine_select(out=upto, in_=ones, compare_op=ALU.is_ge, fill=0.0, base=0,
                                    pattern=[[1, P]], channel_multiplier=-1))
            made(pool.affine_select(out=after, in_=ones, compare_op=ALU.is_gt, fill=0.0, base=0,
                                    pattern=[[-1, P]], channel_multiplier=1))
            made(pool.memset(eps, EPS))
            made(pool.iota(iota_i, pattern=[[1, PK]], base=0, channel_multiplier=0))
            for i in range(HALF):
                made(pool.memset(inv_freq[:, i:i + 1], float(THETA ** (-2.0 * i / HD))))
            made(pool.memset(state, 0.0))
            made(pool.memset(hist.rearrange("p a n -> p (a n)"), 0.0))
            made(pool.memset(causal, 0.0))
            made(pool.affine_select(out=causal, in_=causal, compare_op=ALU.is_ge, fill=NEG, base=7 * P,
                                    pattern=[[-1, SEQ + 7 * P]], channel_multiplier=1))
            pool.sem_inc(s_consts, 1)
            pool.dma_start(convb, conv_b[0].rearrange("(c p) -> p c", p=P), allow_slow_non_contiguous=True).then_inc(s_small, 16)
            pool.dma_start(convw, conv_w[0].rearrange("j (c p) -> p (j c)", p=P),
                           allow_slow_non_contiguous=True).then_inc(s_small, 16)
            pool.dma_start(dtb, dt_bias[0, :].partition_broadcast(P)).then_inc(s_small, 16)
            pool.dma_start(neg_a, a_log[0, :].partition_broadcast(P)).then_inc(s_small, 16)
            pool.dma_start(dskip, d_skip[0, :].partition_broadcast(P)).then_inc(s_small, 16)
            pool.dma_start(keys_raw.rearrange("p h (t d) -> p h t d", t=2),
                           peer_sub_keys[0].rearrange("h t k d -> k h t d")).then_inc(s_keys, 16)
            x_blocks = x.rearrange("o (b p) d -> b p (o d)", p=P)
            for b in range(NB):
                if b:
                    pool.wait_ge(s_sumsq, b)
                pool.dma_start(x1n, x_blocks[b]).then_inc(s_xs, 16)
            pool.wait_ge(s_sumsq, NB)
            pool.dma_start(x1n, x_blocks[0]).then_inc(a_x.sem, 16)
            with pool.Fori(1, NB) as b:
                a_h.wait(pool, b, 0)
                pool.dma_start(x1n, x_blocks[b]).then_inc(a_x.sem, 16)

            def experts(b):
                prep.wait(pool, b, 1)
                dot.wait(pool, b, 0)
                pool.sem_inc(s_room, 1)
                pool.tensor_copy(idxu, idxn).then_inc(idxc.sem, 1)
                idxc.wait(pool, b, 1)
                pool.sem_inc(s_room, 1)
                for n in range(SLOTS + LAG):
                    if n < SLOTS:
                        r = n % UR
                        if n >= UR:
                            dot.wait(pool, b, n - UR + 1)
                            pool.sem_inc(s_room, 1)
                        pool.indirect_dma_start(
                            out=u_ring[r], out_offset=None, in_=peer_u[0],
                            in_offset=bass.IndirectOffsetOnAxis(ap=idxu[:, n:n + 1], axis=0),
                        ).then_inc(u_in[r], 16)
                    m = n - LAG
                    if m >= 0:
                        if m == 0:
                            vused.wait(pool, b, 0)
                            pool.sem_inc(s_room, 1)
                            pool.tensor_copy(idxv, idxn).then_inc(idxc.sem, 1)
                            idxc.wait(pool, b, 2)
                            pool.sem_inc(s_room, 1)
                        r = m % VR
                        if m >= VR:
                            vused.wait(pool, b, m - VR + 1)
                            pool.sem_inc(s_room, 1)
                        pool.indirect_dma_start(
                            out=v_ring[r], out_offset=None, in_=peer_v[0],
                            in_offset=bass.IndirectOffsetOnAxis(ap=idxv[:, m:m + 1], axis=0),
                        ).then_inc(v_in[r], 16)

            experts(0)
            with pool.Fori(1, NB) as b:
                experts(b)

        @block.scalar
        def _(act):
            steps = Steps(act, astep)
            sc = nc.scalar
            act.wait_ge(s_rows, 32)
            sc.activation(scT, scT, ACT.Silu).then_inc(s_silu, 1)
            act.wait_ge(s_consts, 1)
            for b in range(NB):
                act.wait_ge(s_xs, 16 * (b + 1))
                sc.activation(h2n, x1n, ACT.Square, accum_out=rowsum[:, b:b + 1]).then_inc(s_sumsq, 1)
            act.wait_ge(s_sumsq, NB)
            sc.activation(rstd, rowsum, ACT.Sqrt, scale=1.0 / D, bias=eps).then_inc(s_root, 1)
            act.wait_ge(s_small, 16 * 5)
            act.wait_ge(s_ang, 1)
            sc.activation(sinT, sinT, ACT.Sin)
            sc.activation(cosT, cosT, ACT.Sin).then_inc(s_trig, 1)

            def project(b):
                a_hps.wait(act, b, 1)
                sc.copy(hT.rearrange("p a n -> p (a n)"), bank(0, 2)).then_inc(a_hT.sem, 1)
                a_rope.wait(act, b, 0)
                a_out.wait(act, b, 0)
                a_proj.wait(act, b, 1)
                sc.copy(raw[:, 0:512], bank(2))
                a_proj.wait(act, b, 2)
                kk = bank(3)[:, 0:128].rearrange("p (g d) -> p g d", g=2)
                for twice in range(2):
                    sc.copy(raw[:, 1024:1280].rearrange("p (g t d) -> p g t d", g=2, t=2)[:, :, twice, :], kk)
                sc.copy(raw[:, 512:768], bank(3)[:, 256:512])
                sc.copy(vv[:, b, :], bank(3)[:, 128:256])
                a_proj.wait(act, b, 3)
                sc.copy(raw[:, 768:1024], bank(4)[:, 0:256])
                for twice in range(2):
                    last = sc.copy(raw[:, 1280 + 64 * twice:1344 + 64 * twice], bank(4)[:, 256:320])
                last.then_inc(a_raw.sem, 1)
                sc.copy(grid(dtwi, NB)[:, b, :], bank(4)[:, 320:336])
                a_proj.wait(act, b, 4)
                sc.copy(stag[:, 1024:1536], bank(5))
                a_rps.wait(act, b, 1)
                sc.copy(stag[:, 0:512], bank(0))
                sc.copy(stag[:, 512:1024], bank(1))
                for i, kT in enumerate((k0T, k1T, kiT)):
                    last = sc.copy(grid(kT, NB)[:, b, :], bank(2)[:, i * P:(i + 1) * P])
                last.then_inc(a_rot.sem, 1)

            project(0)
            with act.Fori(1, NB) as b:
                project(b)

            act.wait_ge(s_dtv, 1)
            sc.activation(small[:, 0:64], small[:, 0:64], ACT.Exp, scale=-1.0)
            sc.activation(neg_a, neg_a, ACT.Exp).then_inc(s_dta, 1)
            act.wait_ge(s_dtv, 2)
            sc.activation(small[:, 64:128], small[:, 64:128], ACT.Ln).then_inc(s_dta, 1)
            act.wait_ge(s_dtv, 4)
            sc.activation(eac, bank(0)[:, 0:64], ACT.Exp)
            sc.activation(etot, bank(0)[:, 64:128], ACT.Exp)
            sc.activation(dec, small[:, 0:64], ACT.Exp).then_inc(s_dta, 1)

            def root(col, width):
                return sc.activation(stat[:, col:col + 1], stat[:, col:col + 1], ACT.Sqrt,
                                     scale=1.0 / width, bias=eps)

            def mixing(b):
                steps.begin()
                yield 8
                conv.wait(act, b, 1)
                for t in range(CT):
                    sc.activation(cv[:, t, :], cv[:, t, :], ACT.Silu, bias=convb[:, t:t + 1])\
                        .then_inc(convact.sem, 1)
                yield 10
                m_z.wait(act, b, 16)
                sc.activation(zt, zt, ACT.Silu).then_inc(zgate.sem, 1)
                for g in range(2):
                    yield 17 + 2 * g
                    seg.wait(act, b, g + 1)
                    sc.activation(L[:, g * 512:(g + 1) * 512], bank(2 + g), ACT.Exp).then_inc(decay.sem, 1)
                yield 27
                gated.wait(act, b, 1)
                steps(sc.activation(ytmp, yy, ACT.Square, accum_out=stat[:, 0:1]))
                root(0, 512).then_inc(ssdrms.sem, 1)
                for h in range(HEADS):
                    yield 29 + h
                    if h == 0:
                        ssdout.wait(act, b, 1)
                    if h >= 2:
                        scacc.wait(act, b, h - 1)
                    logit.wait(act, b, h + 1)
                    sc.activation(RL[h % 2], SB if h % 2 == 0 else TB, ACT.Relu, scale=HD ** -0.5)\
                        .then_inc(relu.sem, 1)
                for h in range(HEADS + 1):
                    if h < HEADS:
                        yield 118 + 3 * h
                        smax.wait(act, b, h + 1)
                        sc.activation(RL[h % 2], RL[h % 2], ACT.Exp, bias=negmax[:, h:h + 1],
                                      accum_out=psums[:, h:h + 1]).then_inc(sexp.sem, 1)
                    yield 119 + 3 * h
                    if h < HEADS:
                        ptps.wait(act, b, h + 1)
                        if h:
                            av.wait(act, b, h)
                        sc.copy(PT.rearrange("p a n -> p (a n)"), TB).then_inc(ptc.sem, 1)
                yield 148
                outps.wait(act, b, 1)
                steps(sc.activation(otmp, SB, ACT.Square, accum_out=stat[:, 1:2]))
                root(1, D).then_inc(outrms.sem, 1)
                yield 151
                x1r.wait(act, b, 1)
                steps(sc.activation(otmp, x1n, ACT.Square, accum_out=stat[:, 2:3]))
                root(2, D).then_inc(x1rms.sem, 1)
                yield 159
                pqps.wait(act, b, 1)
                sc.copy(qpT.rearrange("p a n -> p (a n)"), SB).then_inc(pqr.sem, 1)
                yield 161
                pss.wait(act, b, 1)
                sc.copy(ss[:, 0:1024], SB).then_inc(s2.sem, 1)
                sc.copy(ss[:, 1024:2048], TB).then_inc(s2.sem, 1)
                yield 196
                fvr.wait(act, b, 1)
                sc.activation(gn, gn, ACT.Exp).then_inc(gexp.sem, 1)

            def experts(b, weave):
                for n in range(SLOTS + LAG):
                    if n % PK == 0 and 0 < n <= SLOTS:
                        h = n // PK - 1
                        s = slice(h * PK, (h + 1) * PK)
                        dot.wait(act, b, n)
                        sc.activation(gel[:, s], dots[:, s], ACT.Gelu).then_inc(gelu.sem, 1)
                    m = n - LAG
                    if m >= 0:
                        wready.wait(act, b, m // PK + 1)
                        if m >= GR:
                            vused.wait(act, b, m - GR + 1)
                        sc.activation(diag[m % GR], ident, ACT.Copy, scale=wgt[:, m:m + 1]).then_inc(dg.sem, 1)
                    if n < SLOTS and weave:
                        weave.upto(slot_stage(n))
                if weave:
                    weave.upto(END - 1)
                vused.wait(act, b + 1, 0)
                sc.activation(h2c, VB, ACT.Square, accum_out=stat[:, 3:4]).then_inc(frsum.sem, 1)
                frsum.wait(act, b, 1)
                root(3, D).then_inc(frms.sem, 1)

            Weave(mixing(0)).upto(END - 1)
            experts(0, Weave(mixing(1)))
            with act.Fori(1, NB - 1) as b:
                experts(b, Weave(mixing(b + 1)))
            experts(NB - 1, None)

        @block.tensor
        def _(pe):
            te = nc.tensor

            def turn(dst, src, tiles):
                for i in range(tiles):
                    last = te.transpose(dst[:, i * P:(i + 1) * P], src[:, i * P:(i + 1) * P], ident)
                return last

            def turn_rows(dst, src, tiles):
                for i in range(tiles):
                    last = te.transpose(dst[:, i * P:(i + 1) * P], src[:, i, :], ident)
                return last

            pe.wait_ge(s_consts, 1)
            pe.wait_ge(s_wide, 1)
            wide = grid(mix, KC)
            for half in range(2):
                pe.wait_ge(s_brow[half], 16)
                if half:
                    pe.wait_ge(s_mod, 1)
                for j in range(6):
                    te.matmul(bank(j), ones[0:1, :], b_row[:, j * 512:(j + 1) * 512], start=True, stop=False)
                for k in range(KC):
                    n = half * KC + k
                    pe.wait_ge(s_ada[n % 3], 16 * (n // 3 + 1))
                    for j in range(6):
                        last = te.matmul(bank(j), wide[:, k, :], ada_buf[n % 3][:, j * 512:(j + 1) * 512],
                                         start=False, stop=(k == KC - 1))
                    last.then_inc(s_adaused, 1)
            pe.wait_ge(s_keys, 16)
            pe.wait_ge(s_mod, 2)
            turn_rows(bank(0, 2), keys_raw, HEADS).then_inc(s_keyps, 1)
            pe.wait_ge(s_keysT, 1)
            pe.wait_ge(s_win, 16 * KC)

            def project(b):
                a_rot.wait(pe, b, 0)
                a_h.wait(pe, b, 1)
                turn(bank(0, 2), h2n, KC).then_inc(a_hps.sem, 1)
                a_hT.wait(pe, b, 1)
                groups = [((2, 0, 512, 0),), ((3, 0, 512, 512),), ((4, 0, C_Z - 1024, 1024), (4, C_Z - 1024, 8, C_DT)),
                          ((5, 0, 512, C_Z),)]
                for parts in groups:
                    for i, at, width, col in parts:
                        for k in range(KC):
                            last = te.matmul(bank(i)[:, at:at + width], hT[:, k, :], w_in_sb[:, k, col:col + width],
                                             start=(k == 0), stop=(k == KC - 1))
                    last.then_inc(a_proj.sem, 1)
                a_xbc.wait(pe, b, 0)
                for t in range(CT):
                    for k in range(KC):
                        last = te.matmul(bank(6 + t // 4)[:, t % 4 * P:(t % 4 + 1) * P],
                                         w_in_sb[:, k, C_XBC + t * P:C_XBC + (t + 1) * P], hT[:, k, :],
                                         start=(k == 0), stop=(k == KC - 1))
                    if t % 4 == 3:
                        last.then_inc(a_proj.sem, 1)
                a_rope.wait(pe, b, 1)
                a_raw.wait(pe, b, 1)
                turn(bank(0, 2), rot, 8)
                turn(bank(2), rot[:, 1024:1408], 3).then_inc(a_rps.sem, 1)

            project(0)
            with pe.Fori(1, NB) as b:
                project(b)

            a_rot.wait(pe, NB, 0)
            pe.wait_ge(s_dtv, 3)
            te.matmul(bank(0)[:, 0:64], upto, adt, start=True, stop=True)
            te.matmul(bank(0)[:, 64:128], ones, adt, start=True, stop=True).then_inc(s_dtp, 1)

            def mixing(b):
                yield 10
                convact.wait(pe, b, CT)
                for t in range(4):
                    last = te.transpose(XB[:, t * P:(t + 1) * P], cv[:, t, :], ident)
                last.then_inc(chanT.sem, 1)
                for t in range(2):
                    last = te.transpose(OB[:, t * P:(t + 1) * P], cv[:, 4 + t, :], ident)
                last.then_inc(chanT.sem, 1)
                for g in range(2):
                    last = te.matmul(bank(4)[:, g * P:(g + 1) * P], cv[:, 4 + g, :], cv[:, 6 + g, :],
                                     start=True, stop=True)
                last.then_inc(cbps.sem, 1)
                for g in range(2):
                    yield 16 + 2 * g
                    ghr.wait(pe, b, g + 1)
                    for i in range(4):
                        last = te.matmul(bank(2 + g)[:, i * P:(i + 1) * P], gh[:, i, :], upto, start=True, stop=True)
                    last.then_inc(seg.sem, 1)
                yield 18
                tok.wait(pe, b, 1)
                stdone.wait(pe, b, 0)
                for g in range(2):
                    last = te.matmul(OB[:, g * 256:(g + 1) * 256], cv[:, 6 + g, :], state[:, g * 256:(g + 1) * 256],
                                     start=True, stop=True)
                last.then_inc(yoff.sem, 1)
                xwr.wait(pe, b, 1)
                for g in range(2):
                    last = te.matmul(XB[:, g * 256:(g + 1) * 256], btok[:, g * P:(g + 1) * P],
                                     xw[:, g * 256:(g + 1) * 256], start=True, stop=True)
                last.then_inc(stps.sem, 1)
                for g in range(2):
                    yield 21 + 2 * g
                    masked.wait(pe, b, g + 1)
                    for h in range(4 * g, 4 * g + 4):
                        last = te.matmul(bank(5)[:, h * HD:(h + 1) * HD], L[:, h * P:(h + 1) * P],
                                         xdt[:, h * HD:(h + 1) * HD], start=True, stop=True)
                last.then_inc(ydiag.sem, 1)
                m_qq.wait(pe, b, 16)
                for h in range(HEADS):
                    yield 28 + h
                    if h == 1:
                        gated.wait(pe, b, 1)
                    if h >= 2:
                        relu.wait(pe, b, h - 1)
                    dst = SB if h % 2 == 0 else TB
                    half = slice(h % 2 * HD, h % 2 * HD + HD)
                    for j in range(2):
                        last = te.matmul(dst[:, j * 512:(j + 1) * 512], qiT[half, h // 2, :],
                                         kiT[half, j * 512:(j + 1) * 512], start=True, stop=True)
                    last.then_inc(logit.sem, 1)

                def scores(h):
                    if h == 0:
                        relu.wait(pe, b, HEADS)
                    else:
                        sread.wait(pe, b, h)
                    half = slice(h % 2 * HD, h % 2 * HD + HD)
                    kT = (k0T, k1T)[h // 4]
                    for j in range(2):
                        last = te.matmul(SB[:, j * 512:(j + 1) * 512], qT[half, h // 2, :],
                                         kT[half, j * 512:(j + 1) * 512], start=True, stop=True)
                    last.then_inc(sps.sem, 1)

                def values(h):
                    ptc.wait(pe, b, h + 1)
                    for j in range(NB):
                        last = te.matmul(OB[:, h * HD:(h + 1) * HD], PT[:, j, :],
                                         vv[:, j, h // 4 * HD:(h // 4 + 1) * HD], start=(j == 0), stop=(j == NB - 1))
                    last.then_inc(av.sem, 1)

                yield 110
                scores(0)
                for h in range(HEADS):
                    yield 118 + 3 * h
                    if h < HEADS - 1:
                        scores(h + 1)
                    sexp.wait(pe, b, h + 1)
                    if h:
                        ptc.wait(pe, b, h)
                    turn(TB, RL[h % 2], NB).then_inc(ptps.sem, 1)
                    yield 120 + 3 * h
                    values(h)
                yield 144
                mixr.wait(pe, b, 1)
                turn(TB, mix, KC).then_inc(mixps.sem, 1)
                for j in range(2):
                    yield 146 + j
                    mixTr.wait(pe, b, 1)
                    if j == 0:
                        pe.wait_ge(s_wout, 16)
                    for k in range(KC):
                        last = te.matmul(SB[:, j * 512:(j + 1) * 512], mixT[:, k, :],
                                         w_out_sb[:, k, j * 512:(j + 1) * 512], start=(k == 0), stop=(k == KC - 1))
                last.then_inc(outps.sem, 1)
                yield 155
                h2r.wait(pe, b, 1)
                turn(TB, h2n, KC).then_inc(h2ps.sem, 1)
                for h in range(HEADS):
                    yield 157 + h // 4
                    if h == 0:
                        h2Tr.wait(pe, b, 1)
                        pe.wait_ge(s_wq, 16)
                    for k in range(KC):
                        last = te.matmul(SB[:, h * P:(h + 1) * P], w_q_sb[:, k, h * P:(h + 1) * P], h2T[:, k, :],
                                         start=(k == 0), stop=(k == KC - 1))
                last.then_inc(pqps.sem, 1)
                yield 160
                pqr.wait(pe, b, 1)
                for i in range(LISTS):
                    half = slice(i // HEADS * HD, i // HEADS * HD + HD)
                    last = te.matmul(bank(2 + i // 4)[:, i % 4 * P:(i % 4 + 1) * P], qpT[half, i % HEADS, :],
                                     keysT[half, i % HEADS, :], start=True, stop=True)
                last.then_inc(pss.sem, 1)

            def experts(b, weave):
                for n in range(SLOTS + LAG):
                    m = n - LAG
                    if m >= 0:
                        r = m % VR
                        if m == 0:
                            fread.wait(pe, b, 0)
                        dg.wait(pe, b, m + 1)
                        pe.wait_ge(v_in[r], 16 * (b * uses(VR, r) + m // VR + 1))
                        for j in range(2):
                            last = te.matmul(VB[:, j * 512:(j + 1) * 512], diag[m % GR],
                                             v_ring[r][:, j * 512:(j + 1) * 512], start=(m == 0), stop=(m == SLOTS - 1))
                        last.then_inc(vused.sem, 1)
                    if n < SLOTS and weave:
                        weave.upto(slot_stage(n))
                if weave:
                    weave.upto(END - 1)

            Weave(mixing(0)).upto(END - 1)
            experts(0, Weave(mixing(1)))
            with pe.Fori(1, NB - 1) as b:
                experts(b, Weave(mixing(b + 1)))
            experts(NB - 1, None)

        @block.vector
        def _(vec):
            ve = nc.vector
            setup = Steps(vec, bstep)
            steps = Steps(vec, vstep)
            pert = Steps(vec, pstep)
            ropes = Steps(vec, rstep)

            vec.wait_ge(s_silu, 1)
            ve.tensor_copy(grid(mix, KC), over_last(scT, P)).then_inc(s_wide, 1)
            vec.wait_ge(s_consts, 1)
            vec.wait_ge(s_rows, 32)
            setup(ve.tensor_copy(iota16, iota_i))
            setup(ve.tensor_copy(pos_f, pos_i))
            setup(ve.tensor_tensor(grid(ang, NB), over_last(pos_f, HALF), over_first(inv_freq, NB), ALU.mult))
            RND = 12582912.0
            C1 = 6.28125
            C2 = float(2 * math.pi - 6.28125)
            PI = 3.1415925
            setup(ve.tensor_scalar(ang2, ang, 1.0 / (2 * math.pi), RND, ALU.mult, ALU.add))
            setup(ve.tensor_scalar(ang2, ang2, -RND, None, ALU.add))
            setup(ve.scalar_tensor_tensor(out=ang, in0=ang2, scalar=-C1, in1=ang, op0=ALU.mult, op1=ALU.add))
            setup(ve.scalar_tensor_tensor(out=ang, in0=ang2, scalar=-C2, in1=ang, op0=ALU.mult, op1=ALU.add))
            setup(ve.tensor_scalar(sinT, ang, PI, -PI, ALU.min, ALU.max))
            setup(ve.tensor_scalar(ang, ang, math.pi / 2, None, ALU.add))
            setup(ve.tensor_scalar(ang2, ang, math.pi, -2 * math.pi, ALU.is_gt, ALU.mult))
            setup(ve.tensor_tensor(ang, ang, ang2, ALU.add))
            ve.tensor_scalar(cosT, ang, PI, -PI, ALU.min, ALU.max).then_inc(s_ang, 1)
            vec.wait_ge(s_root, 1)
            setup(ve.reciprocal(rstd, rstd))
            vec.wait_ge(s_small, 16 * 5)
            vec.wait_ge(s_gain, 16 * 5)
            vec.wait_ge(s_adaused, KC)
            ve.tensor_copy(B1, bank(0, 2))
            ve.scalar_tensor_tensor(out=A1, in0=bank(2, 2), scalar=1.0, in1=A1, op0=ALU.add, op1=ALU.mult)
            ve.tensor_tensor(P1, bank(4, 2), P1, ALU.mult).then_inc(s_mod, 1)
            vec.wait_ge(s_adaused, 2 * KC)
            ve.tensor_copy(B2, bank(0, 2))
            ve.scalar_tensor_tensor(out=A2, in0=bank(2, 2), scalar=1.0, in1=A2, op0=ALU.add, op1=ALU.mult)
            ve.tensor_tensor(P2, bank(4, 2), P2, ALU.mult).then_inc(s_mod, 1)
            vec.wait_ge(s_mod, 2)
            vec.wait_ge(s_keyps, 1)
            ve.tensor_copy(keysT.rearrange("p a n -> p (a n)"), bank(0, 2)).then_inc(s_keysT, 1)
            vec.wait_ge(s_trig, 1)

            heads = 22
            def project(b):
                ropes.begin()
                a_x.wait(vec, b, 16)
                a_hps.wait(vec, b, 0)
                ropes(ve.scalar_tensor_tensor(out=h2n, in0=x1n, scalar=rstd[:, bass.ds(b, 1)], in1=A1,
                                              op0=ALU.mult, op1=ALU.mult))
                ve.tensor_tensor(h2n, h2n, B1, ALU.add).then_inc(a_h.sem, 1)
                a_raw.wait(vec, b, 1)
                a_rps.wait(vec, b, 0)
                r3, o3, t3 = grid(raw, heads), grid(rot, heads), grid(rtmp, heads)
                cos = over_first(grid(cosT, NB)[:, b, :], heads)
                sin = over_first(grid(sinT, NB)[:, b, :], heads)
                x1, x2 = r3[:, :, 0:HALF], r3[:, :, HALF:HD]
                ropes(ve.tensor_tensor(t3, x2, sin, ALU.mult))
                ropes(ve.tensor_tensor(o3[:, :, 0:HALF], x1, cos, ALU.mult))
                ropes(ve.tensor_tensor(o3[:, :, 0:HALF], o3[:, :, 0:HALF], t3, ALU.subtract))
                ropes(ve.tensor_tensor(t3, x1, sin, ALU.mult))
                ropes(ve.tensor_tensor(o3[:, :, HALF:HD], x2, cos, ALU.mult))
                ve.tensor_tensor(o3[:, :, HALF:HD], o3[:, :, HALF:HD], t3, ALU.add).then_inc(a_rope.sem, 1)
                a_proj.wait(vec, b, 6)
                a_out.wait(vec, b, 0)
                ve.tensor_copy(stag[:, 1536:2560], bank(6, 2)).then_inc(a_xbc.sem, 1)

            project(0)
            with vec.Fori(1, NB) as b:
                project(b)

            small3 = [small[:, i * 64:(i + 1) * 64] for i in range(6)]
            a_rot.wait(vec, NB, 0)
            dw = grid(dtwi, NB)
            setup(ve.tensor_scalar(grid(wis, NB), dw[:, :, 0:8], float(HEADS ** -0.5), None, ALU.mult))
            setup(ve.tensor_tensor(grid(small3[2], NB), dw[:, :, 8:16], over_first(dtb, NB), ALU.add))
            setup(ve.tensor_scalar(small3[3], small3[2], 0.0, None, ALU.max))
            setup(ve.tensor_scalar(small3[4], small3[2], -1.0, None, ALU.mult))
            ve.tensor_tensor(small3[0], small3[2], small3[4], ALU.max).then_inc(s_dtv, 1)
            vec.wait_ge(s_dta, 1)
            setup(ve.tensor_scalar(neg_a, neg_a, -1.0, None, ALU.mult))
            setup(ve.tensor_scalar(small3[1], small3[0], 1.0, None, ALU.add))
            setup(ve.tensor_scalar(small3[2], small3[1], -1.0, None, ALU.add))
            setup(ve.tensor_scalar(small3[4], small3[2], 1e-30, None, ALU.max))
            setup(ve.reciprocal(small3[4], small3[4]))
            ve.tensor_tensor(small3[4], small3[4], small3[0], ALU.mult).then_inc(s_dtv, 1)
            vec.wait_ge(s_dta, 2)
            setup(ve.tensor_tensor(small3[4], small3[4], small3[1], ALU.mult))
            setup(ve.scalar_tensor_tensor(out=small3[5], in0=small3[2], scalar=0.0, in1=small3[0],
                                          op0=ALU.is_equal, op1=ALU.mult))
            setup(ve.tensor_tensor(small3[4], small3[4], small3[5], ALU.add))
            setup(ve.tensor_tensor(dt_s, small3[4], small3[3], ALU.add))
            ve.tensor_tensor(grid(adt, NB), grid(dt_s, NB), over_first(neg_a, NB), ALU.mult).then_inc(s_dtv, 1)
            vec.wait_ge(s_dtp, 1)
            setup(ve.tensor_copy(small3[0], bank(0)[:, 64:128]))
            ve.tensor_tensor(small3[0], small3[0], bank(0)[:, 0:64], ALU.subtract).then_inc(s_dtv, 1)
            vec.wait_ge(s_dta, 3)

            def mixing(b):
                steps.begin()
                yield 0
                m_xbc.wait(vec, b, 16)
                steps(ve.tensor_copy(xc[:, :, 0:3], hist))
                w3 = grid(convw, TAPS)
                steps(ve.tensor_tensor(cv, xc[:, :, 3:131], over_last(w3[:, 3, :], P), ALU.mult))
                for j in range(3):
                    yield 2 + 2 * j
                    steps(ve.tensor_tensor(ctmp, xc[:, :, j:j + P], over_last(w3[:, j, :], P),
                                           ALU.mult))
                    yield 3 + 2 * j
                    if j < 2:
                        steps(ve.tensor_tensor(cv, cv, ctmp, ALU.add))
                    else:
                        ve.tensor_tensor(cv, cv, ctmp, ALU.add).then_inc(conv.sem, 1)
                steps(ve.tensor_copy(hist, xc[:, :, 128:131]))
                adt_b, dt_b = grid(adt, NB)[:, b, :], grid(dt_s, NB)[:, b, :]
                yield 9
                ve.tensor_tensor(gh, over_first(after, 4), over_last(adt_b[:, 0:4], P), ALU.mult)\
                    .then_inc(ghr.sem, 1)
                yield 12
                chanT.wait(vec, b, 2)
                steps(ve.tensor_copy(xtok, XB))
                steps(ve.tensor_tensor(grid(xdt, HEADS), grid(XB, HEADS), over_last(dt_b, HD), ALU.mult))
                ve.tensor_copy(btok, OB[:, 0:256]).then_inc(tok.sem, 1)
                yield 14
                ve.tensor_tensor(grid(xw, HEADS), grid(xdt, HEADS), over_last(grid(dec, NB)[:, b, :], HD),
                                 ALU.mult).then_inc(xwr.sem, 1)
                cbps.wait(vec, b, 1)
                steps(ve.tensor_tensor(cbm, bank(4)[:, 0:256].rearrange("p (g n) -> p g n", g=2),
                                       over_first(upto, 2), ALU.mult))
                yield 17
                seg.wait(vec, b, 1)
                ve.tensor_tensor(gh, over_first(after, 4), over_last(adt_b[:, 4:8], P), ALU.mult)\
                    .then_inc(ghr.sem, 1)
                for g in range(2):
                    yield 19 + 2 * g
                    decay.wait(vec, b, g + 1)
                    lg = grid(L[:, g * 512:(g + 1) * 512], 4)
                    ve.tensor_tensor(lg, lg, over_first(cbm[:, g, :], 4), ALU.mult).then_inc(masked.sem, 1)
                yield 23
                yoff.wait(vec, b, 1)
                steps(ve.tensor_tensor(grid(yy, HEADS), grid(OB, HEADS), over_last(grid(eac, NB)[:, b, :], HD),
                                       ALU.mult))
                steps(ve.tensor_tensor(grid(state, HEADS), grid(state, HEADS),
                                       over_last(grid(etot, NB)[:, b, :], HD), ALU.mult))
                stps.wait(vec, b, 1)
                ve.tensor_tensor(state, state, XB, ALU.add).then_inc(stdone.sem, 1)
                yield 25
                ydiag.wait(vec, b, 1)
                steps(ve.tensor_tensor(yy, yy, bank(5), ALU.add))
                steps(ve.tensor_tensor(grid(ytmp, HEADS), grid(xtok, HEADS), over_last(dskip, HD), ALU.mult))
                steps(ve.tensor_tensor(yy, yy, ytmp, ALU.add))
                zgate.wait(vec, b, 1)
                ve.tensor_tensor(yy, yy, zt, ALU.mult).then_inc(gated.sem, 1)
                yield 28
                ssdrms.wait(vec, b, 1)
                steps(ve.reciprocal(stat[:, 0:1], stat[:, 0:1]))
                ve.scalar_tensor_tensor(out=mix[:, 512:1024], in0=yy, scalar=stat[:, 0:1], in1=ssdg,
                                        op0=ALU.mult, op1=ALU.mult).then_inc(ssdout.sem, 1)
                wb = grid(wis, NB)[:, b, :]
                for h in range(HEADS):
                    yield 30 + h
                    relu.wait(vec, b, h + 1)
                    if h == 0:
                        ve.tensor_scalar(SC, RL[0], wb[:, 0:1], None, ALU.mult).then_inc(scacc.sem, 1)
                    else:
                        scacc.wait(vec, b, h)
                        ve.scalar_tensor_tensor(out=SC, in0=RL[h % 2], scalar=wb[:, h:h + 1], in1=SC,
                                                op0=ALU.mult, op1=ALU.add).then_inc(scacc.sem, 1)
                yield 38
                scacc.wait(vec, b, HEADS)
                vec.sem_inc(s_turn, 1)
                mask = causal[:, bass.ds((NB - 1 - b) * P, SEQ)]
                steps(ve.tensor_tensor(SC, SC, mask, ALU.add))
                for i in range(TOPK // 8):
                    yield 39 + i * 74 // 32
                    steps(ve.max(mx8, SC))
                    yield 40 + i * 74 // 32
                    steps(ve.match_replace(SC, mx8, SC, TAKEN))
                yield 113
                steps(ve.tensor_scalar(AM, SC, LOW, NEG, ALU.is_gt, ALU.mult))
                yield 115
                steps(ve.tensor_tensor(AM, AM, mask, ALU.add))
                for h in range(HEADS):
                    yield 116 + 3 * h
                    sps.wait(vec, b, h + 1)
                    if h >= 2:
                        ptps.wait(vec, b, h - 1)
                    ve.scalar_tensor_tensor(out=RL[h % 2], in0=SB, scalar=HD ** -0.5, in1=AM,
                                            op0=ALU.mult, op1=ALU.add).then_inc(sread.sem, 1)
                    yield 117 + 3 * h
                    sread.wait(vec, b, h + 1)
                    ve.tensor_reduce(negmax[:, h:h + 1], RL[h % 2], AX.X, ALU.max, negate=True)\
                        .then_inc(smax.sem, 1)
                yield 143
                av.wait(vec, b, HEADS)
                steps(ve.reciprocal(rsums, psums))
                ve.tensor_tensor(grid(mix[:, 0:512], HEADS), grid(OB, HEADS), over_last(rsums, HD), ALU.mult)\
                    .then_inc(mixr.sem, 1)
                yield 145
                mixps.wait(vec, b, 1)
                ve.tensor_copy(mixT.rearrange("p a n -> p (a n)"), TB).then_inc(mixTr.sem, 1)
                yield 149
                outrms.wait(vec, b, 1)
                m_x.wait(vec, b, 16)
                steps(ve.reciprocal(stat[:, 1:2], stat[:, 1:2]))
                steps(ve.scalar_tensor_tensor(out=otmp, in0=SB, scalar=stat[:, 1:2], in1=P1,
                                              op0=ALU.mult, op1=ALU.mult))
                yield 150
                ve.tensor_tensor(x1n, x1n, otmp, ALU.add).then_inc(x1r.sem, 1)
                yield 152
                x1rms.wait(vec, b, 1)
                steps(ve.reciprocal(stat[:, 2:3], stat[:, 2:3]))
                steps(ve.scalar_tensor_tensor(out=h2n, in0=x1n, scalar=stat[:, 2:3], in1=A2,
                                              op0=ALU.mult, op1=ALU.mult))
                yield 154
                ve.tensor_tensor(h2n, h2n, B2, ALU.add).then_inc(h2r.sem, 1)
                yield 156
                h2ps.wait(vec, b, 1)
                ve.tensor_copy(h2T.rearrange("p a n -> p (a n)"), TB).then_inc(h2Tr.sem, 1)
                for i in range(LISTS):
                    yield 162 + i
                    if i % 8 == 0:
                        s2.wait(vec, b, i // 8 + 1)
                        vec.sem_inc(s_turn, 1)
                    s = ss[:, i * P:(i + 1) * P]
                    lo, hi = slice(i * PK, i * PK + 8), slice(i * PK + 8, (i + 1) * PK)
                    steps(ve.max(sv[:, lo], s))
                    steps(ve.max_index(si[:, lo], sv[:, lo], s))
                    steps(ve.match_replace(s, sv[:, lo], s, TAKEN))
                    steps(ve.max(sv[:, hi], s))
                    steps(ve.max_index(si[:, hi], sv[:, hi], s))
                yield 178
                steps(ve.tensor_copy(sif, si))
                sv4 = sv.rearrange("p (t h k) -> p t h k", h=HEADS, t=2)
                cand4 = cand.rearrange("p (h i j) -> p h i j", h=HEADS, i=PK)
                for h in range(HEADS):
                    steps(ve.tensor_tensor(cand4[:, h], over_last(sv4[:, 0, h], PK), over_first(sv4[:, 1, h], PK),
                                           ALU.add))
                for h in range(HEADS):
                    yield 181 + 2 * h
                    cd = cand[:, h * 256:(h + 1) * 256]
                    lo, hi = slice(h * PK, h * PK + 8), slice(h * PK + 8, (h + 1) * PK)
                    steps(ve.max(fv[:, lo], cd))
                    steps(ve.max_index(fp[:, lo], fv[:, lo], cd))
                    steps(ve.match_replace(cd, fv[:, lo], cd, TAKEN))
                    steps(ve.max(fv[:, hi], cd))
                    steps(ve.max_index(fp[:, hi], fv[:, hi], cd))
                yield 195
                steps(ve.tensor_reduce(gsum, grid(fv, HEADS), AX.X, ALU.max))
                ve.tensor_tensor(grid(gn, HEADS), grid(fv, HEADS), over_last(gsum, PK), ALU.subtract)\
                    .then_inc(fvr.sem, 1)
                idxc.wait(vec, b, 0)
                hot3 = hot.rearrange("p (n k) -> p n k", k=PK)
                for t in range(2):
                    yield 197 + 4 * t
                    if t == 0:
                        steps(ve.tensor_scalar(fpi, fp, 4, None, ALU.logical_shift_right))
                    else:
                        steps(ve.tensor_scalar(fpi, fp, 15, None, ALU.bitwise_and))
                    steps(ve.tensor_copy(fpf, fpi))
                    steps(ve.tensor_tensor(hot3, over_first(iota16, SLOTS), over_last(fpf, PK), ALU.is_equal))
                    yield 199 + 4 * t
                    sif4 = sif.rearrange("p (t h k) -> p t h k", h=HEADS, t=2)
                    for h in range(HEADS):
                        hh = hot3[:, h * PK:(h + 1) * PK, :]
                        steps(ve.tensor_tensor(hh, hh, over_first(sif4[:, t, h], PK), ALU.mult))
                    steps(ve.tensor_reduce((e1, fpf)[t], hot3, AX.X, ALU.add))
                steps(ve.scalar_tensor_tensor(out=e1, in0=e1, scalar=float(EXPERT_KEYS), in1=fpf,
                                              op0=ALU.mult, op1=ALU.add))
                steps(ve.tensor_copy(idxn, e1))
                gexp.wait(vec, b, 1)
                steps(ve.tensor_reduce(gsum, grid(gn, HEADS), AX.X, ALU.add))
                steps(ve.reciprocal(gsum, gsum))
                ve.tensor_tensor(grid(gn, HEADS), grid(gn, HEADS), over_last(gsum, PK), ALU.mult)\
                    .then_inc(prep.sem, 1)

            def experts(b, weave):
                pert.begin()
                prep.wait(vec, b, 1)
                xfin.wait(vec, b, 0)
                ve.tensor_copy(gc, gn)
                pert(ve.tensor_copy(h2c, h2n))
                for n in range(SLOTS + 2):
                    if n < SLOTS:
                        r = n % UR
                        vec.wait_ge(u_in[r], 16 * (b * uses(UR, r) + n // UR + 1))
                        ve.tensor_tensor_reduce(u_ring[r], u_ring[r], h2c, 1.0, 0.0, ALU.mult, ALU.add,
                                                dots[:, n:n + 1]).then_inc(dot.sem, 1)
                    if n % PK == 1 and n > 1:
                        h = n // PK - 1
                        s = slice(h * PK, (h + 1) * PK)
                        gelu.wait(vec, b, h + 1)
                        ve.tensor_tensor(wgt[:, s], gel[:, s], gc[:, s], ALU.mult).then_inc(wready.sem, 1)
                    if n == 2:
                        xout.wait(vec, b, 0)
                        ve.tensor_copy(x1c, x1n).then_inc(xcommit.sem, 1)
                    if n < SLOTS and weave:
                        weave.upto(slot_stage(n))
                if weave:
                    weave.upto(END - 1)
                frms.wait(vec, b, 1)
                pert(ve.reciprocal(stat[:, 3:4], stat[:, 3:4]))
                ve.scalar_tensor_tensor(out=h2c, in0=VB, scalar=stat[:, 3:4], in1=P2,
                                        op0=ALU.mult, op1=ALU.mult).then_inc(fread.sem, 1)
                fread.wait(vec, b, 1)
                ve.tensor_tensor(x1c, x1c, h2c, ALU.add).then_inc(xfin.sem, 1)

            Weave(mixing(0)).upto(END - 1)
            experts(0, Weave(mixing(1)))
            with vec.Fori(1, NB - 1) as b:
                experts(b, Weave(mixing(b + 1)))
            experts(NB - 1, None)


_INS = ['x', 'c', 'positions', 'w_ada', 'b_ada', 'pre_mix_g', 'post_mix_g', 'w_in', 'conv_w', 'conv_b', 'dt_bias',
        'a_log', 'd_skip', 'ssd_norm_g', 'w_out', 'pre_ffn_g', 'post_ffn_g', 'peer_w_q', 'peer_sub_keys',
        'peer_u', 'peer_v']


def kernel(**inputs):
    import numpy as _np
    import concourse.bacc as _bacc
    from concourse import mybir as _mybir
    from concourse.bass_utils import run_bass_kernel_spmd as _run

    nc = _bacc.Bacc("TRN2", target_bir_lowering=False, num_devices=1)
    arrays, args = {}, []
    for name in _INS:
        a = _np.ascontiguousarray(inputs[name])
        arrays[f"in_{name}"] = a
        args.append(nc.dram_tensor(f"in_{name}", a.shape, _mybir.dt.from_np(a.dtype), kind="ExternalInput").ap())
    res = nc.dram_tensor("out_x", (1, SEQ, D), F32, kind="ExternalOutput").ap()
    hybrid_block(nc, *args, res)
    r = _run(nc, [arrays], core_ids=[0])
    return r.results[0]["out_x"]
```

```python
import math
from contextlib import ExitStack

import concourse.bass as bass
from concourse import mybir

ALU = mybir.AluOpType
ACT = mybir.ActivationFunctionType
AX = mybir.AxisListType
F32 = mybir.dt.float32
BF16 = mybir.dt.bfloat16
I32 = mybir.dt.int32
U32 = mybir.dt.uint32

P = 128
D = 1024
KC = D // P
SEQ = 1024
NB = SEQ // P
HD = 64
HEADS = 8
HALF = HD // 2
TOPK = 256
NSTATE = 128
CT = 8
TAPS = 4
EXPERT_KEYS = 128
PK = 16
LISTS = 2 * HEADS
SLOTS = HEADS * PK
THETA = 10000.0
EPS = 1e-6

C_QI = 768
C_KI = 1280
C_Z = 1352
C_XBC = 1864
C_DT = 2888
D_IN = 2896

NEG = -1e30
TAKEN = -3e38
LOW = -2e38

UR = 6
VR = 4
GR = 4
SHORT = TOPK // P
V_USED = SLOTS + 1
END = 1 << 30

PHASES = ((-1, 6, 4, 0), (28, 8, 14, 0), (38, 8, 4, 0), (116, 12, 46, 0), (117, 8, 0, 0), (144, 34, 0, 14),
          (149, 12, 0, 3), (156, 5, 0, 4), (160, 11, 0, 3), (162, 3, 0, 3), (206, 21, 0, 33))
LAST_PHASES = ((0, 17, 68, 0), (0, 8, 0, 0), (0, 103, 0, 93), (0, 0, 0, 35))
LEFT = sum(w for _, _, w, _ in PHASES)


def plan(phases, first=False):
    steps, done, stage = [], [0, 0, 0], -2.0
    for end, *counts in phases:
        base, total = list(done), sum(counts)
        for i in range(total):
            k = max(range(3), key=lambda k: (base[k] - done[k] + counts[k] * (i + 1) / total, -k))
            slot = done[k] + (SLOTS - LEFT if k == 1 else 0)
            done[k] += 1
            if not (first and k == 1):
                steps.append(("uwv"[k], slot, stage + (end - stage) * (i + 1) / total))
        stage = float(end)
    assert done[0] == SLOTS and done[1] == LEFT
    return steps


def moments(steps):
    at = {}
    for i, (kind, slot, _) in enumerate(steps):
        if kind == "u" and slot % PK == PK - 1:
            at.setdefault(i + 1, []).append(("gelu", slot // PK))
            at.setdefault(i + 4, []).append(("weights", slot // PK))
        if kind == "v" and slot % PK == 0:
            assert any(("weights", slot // PK) in at.get(j, ()) for j in range(i + 1)), slot
    first_v = next(i for i, step in enumerate(steps) if step[0] == "v")
    last_w = max([i for i, step in enumerate(steps) if step[0] == "w"] + [first_v - 9])
    at.setdefault(last_w + 1, []).append(("sum", 0))
    at.setdefault(last_w + 5, []).append(("finish", 0))
    at.setdefault(last_w + 14, []).append(("commit", 0))
    return at


class Signal:

    def __init__(self, sem, per=1, first=0):
        self.sem = sem
        self.per = per
        self.first = first

    def at(self, b, k):
        return b * self.per + (k - self.first * self.per)

    def wait(self, eng, b, k):
        value = self.at(b, k)
        if not (isinstance(value, int) and value == 0):
            eng.wait_ge(self.sem, value)


class Steps:

    def __init__(self, eng, sem):
        self.eng, self.sem, self.n = eng, sem, 0

    def begin(self):
        self.eng.sem_clear(self.sem)
        self.n = 0

    def __call__(self, ins):
        self.n += 1
        ins.then_inc(self.sem, 1)
        self.eng.wait_ge(self.sem, self.n)


class Weave:

    def __init__(self, gen):
        self.gen = gen
        self.stage = next(gen, END)

    def upto(self, stage):
        while self.stage <= stage:
            self.stage = next(self.gen, END)


def uses(ring, r):
    return len(range(r, SLOTS, ring))


def hybrid_block(nc, x, c, positions, w_ada, b_ada, pre_mix_g, post_mix_g, w_in, conv_w, conv_b, dt_bias,
                 a_log, d_skip, ssd_norm_g, w_out, pre_ffn_g, post_ffn_g, peer_w_q, peer_sub_keys,
                 peer_u, peer_v, out):
    ctx = ExitStack()
    with ctx:
        def sb(name, cols, dt=F32):
            return ctx.enter_context(nc.sbuf_tensor(name, [P, cols], dt))[:, :]

        def sem(name):
            return ctx.enter_context(nc.semaphore(name))

        def sig(name, per=1, first=0):
            return Signal(sem(name), per, first)

        def grid(ap, a):
            return ap.rearrange("p (a n) -> p a n", a=a)

        def over_last(ap, n):
            return ap.unsqueeze(2).to_broadcast([P, ap.shape[1], n])

        def over_first(ap, n):
            return ap.unsqueeze(1).to_broadcast([P, n, ap.shape[1]])

        ident = sb("ident", P)
        upto = sb("upto", P)
        after = sb("after", P)
        ones = sb("ones", P)
        causal = sb("causal", SEQ + 7 * P, BF16)
        iota_i = sb("iota_i", PK, I32)
        iota16 = sb("iota16", PK)
        inv_freq = sb("inv_freq", HALF)
        pos_i = sb("pos_i", NB, I32)
        pos_f = sb("pos_f", NB)
        eps = sb("eps", 1)
        convw = sb("convw", CT * TAPS)
        convb = sb("convb", CT)
        dtb = sb("dtb", HEADS)
        neg_a = sb("neg_a", HEADS)
        dskip = sb("dskip", HEADS)
        ssdg = sb("ssdg", 512)
        P1 = sb("P1", D)
        A2 = sb("A2", D)
        B2 = sb("B2", D)
        P2 = sb("P2", D)
        KV = sb("KV", 4 * SEQ)
        k0T, k1T, kiT = (KV[:, i * SEQ:(i + 1) * SEQ] for i in range(3))
        vv = grid(KV[:, 3 * SEQ:4 * SEQ], NB)
        keysT = grid(sb("keysT", HEADS * P), HEADS)
        W = sb("W", 16384 + 7168)
        w_in_sb = grid(W[:, 0:KC * D_IN], KC)
        w_out_sb = grid(W[:, 0:8192], KC)
        w_q_sb = grid(W[:, 8192:16384], KC)
        T = W[:, 16384:16384 + 7168]
        ring = sb("ring", (UR + VR) * D)
        u_ring = [ring[:, i * D:(i + 1) * D] for i in range(UR)]
        v_ring = [ring[:, (UR + i) * D:(UR + i + 1) * D] for i in range(VR)]
        diag = [sb(f"diag{i}", P) for i in range(GR)]
        HX = sb("HX", 4 * D)
        h2c, x1c, h2n, x1n = (HX[:, i * D:(i + 1) * D] for i in range(4))
        A1, B1 = h2c, x1c
        mix = sb("mix", D)
        state = sb("state", 512)
        hist = grid(sb("hist", CT * 3), CT)
        rowsum = sb("rowsum", NB)
        rstd = sb("rstd", NB)
        dtwi = sb("dtwi", NB * 16)
        dt_s = sb("dt_s", 64)
        adt = sb("adt", 64)
        eac = sb("eac", 64)
        dec = sb("dec", 64)
        etot = sb("etot", 64)
        wis = sb("wis", 64)
        scT = sb("scT", KC)
        stat = sb("stat", 16)
        negmax = sb("negmax", HEADS)
        psums = sb("psums", HEADS)
        rsums = sb("rsums", HEADS)
        mx8 = sb("mx8", 8)
        idxn = sb("idxn", SLOTS, U32)
        gn = sb("gn", SLOTS)
        idxu = sb("idxu", SLOTS, U32)
        idxv = sb("idxv", SLOTS, U32)
        gc = sb("gc", SLOTS)
        gsum = sb("gsum", HEADS)
        dots = sb("dots", SLOTS)
        gel = sb("gel", SLOTS)
        wgt = sb("wgt", SLOTS)

        ada_buf = [ring[:, i * 3072:(i + 1) * 3072] for i in range(3)]
        b_row = KV[0:1, 0:3072]
        keys_raw = grid(KV[:, 3072:4096], HEADS)
        cosT = ring[:, 9216:9472]
        sinT = ring[:, 9472:9728]
        ang = ring[:, 9728:9984]
        ang2 = ring[:, 9984:10240]
        hT = grid(ring[:, 0:D], KC)
        stag = ring[:, D:D + 2560]
        raw = ring[:, 3584:4992]
        rot = ring[:, 4992:6400]
        rtmp = mix[:, 0:704]
        small = T[:, 4480:4480 + 6 * 64]
        qT = grid(T[:, 0:512], 4)
        qiT = grid(T[:, 512:1024], 4)
        xc = grid(T[:, 1024:1024 + CT * 131], CT)
        L = T[:, 1024:2048]
        cv = grid(T[:, 2072:3096], CT)
        ctmp = grid(T[:, 3096:4120], CT)
        xtok = T[:, 3096:3608]
        btok = T[:, 3608:3864]
        xdt = T[:, 3864:4376]
        xw = T[:, 4376:4888]
        gh = grid(T[:, 4888:5400], 4)
        yy = T[:, 5400:5912]
        ytmp = T[:, 5912:6424]
        cbm = grid(T[:, 6424:6680], 2)
        zt = mix[:, 512:1024]
        SC = T[:, 1024:2048]
        AM = T[:, 2048:3072]
        RL = [T[:, 3072:4096], T[:, 4096:5120]]
        PT = grid(T[:, 5120:6144], NB)
        mixT = grid(T[:, 0:1024], KC)
        otmp = T[:, 1024:2048]
        h2T = grid(T[:, 2048:3072], KC)
        qpT = grid(T[:, 3072:4096], HEADS)
        ss = T[:, 4096:6144]
        cand = T[:, 0:2048]
        hot = T[:, 2048:4096]
        sv = T[:, 6144:6400]
        si = T[:, 6400:6656].bitcast(U32)
        sif = T[:, 6656:6912]
        fv = T[:, 6912:7040]
        fp = T[:, 7040:7168].bitcast(U32)
        fpi = T[:, 4096:4224].bitcast(U32)
        fpf = T[:, 4224:4352]
        e1 = T[:, 4352:4480]

        ps = ctx.enter_context(nc.psum_tensor("ps", [P, 8 * 512], F32))[:, :]

        def bank(i, n=1):
            return ps[:, i * 512:(i + n) * 512]

        VB, SB, TB, OB, XB = bank(0, 2), bank(2, 2), bank(4, 2), bank(6), bank(7)

        spill = nc.dram_tensor("spill", [NB, P, 2560], F32, kind="Internal").ap()

        s_consts = sem("consts_ready")
        s_conststep = sem("const_steps")
        s_small = sem("small_in")
        s_rows = sem("c_positions_in")
        s_gain = sem("gain_in")
        s_brow = [sem("b_ada_in0"), sem("b_ada_in1")]
        s_keys = sem("keys_in")
        s_ada = [sem(f"ada_in{i}") for i in range(3)]
        s_xs = sem("x_stat_in")
        s_sumsq = sem("x_sumsq")
        s_wide = sem("silu_c_wide")
        s_silu = sem("silu_c")
        s_adaused = sem("ada_used")
        s_mod = sem("mod_done")
        s_keyps = sem("keys_psum")
        s_keysT = sem("keys_T")
        s_ang = sem("angles_ready")
        s_trig = sem("trig_ready")
        s_root = sem("x_root")
        s_win = sem("w_in_in")
        s_wout = sem("w_out_in")
        s_wq = sem("w_q_in")

        a_x = sig("a_x_in", 16)
        a_h = sig("a_h")
        a_hps = sig("a_hT_psum")
        a_hT = sig("a_hT")
        a_proj = sig("a_proj", 6)
        a_raw = sig("a_raw")
        a_rope = sig("a_rope")
        a_rps = sig("a_rot_psum")
        a_rot = sig("a_rot")
        a_xbc = sig("a_xbc")
        a_out = sig("a_spilled", 16)
        s_dtv = sem("dt_vector")
        s_dta = sem("dt_scalar")
        s_dtp = sem("dt_psum")

        m_xbc = sig("m_xbc_in", 16)
        m_z = sig("m_z_in", 16)
        m_qq = sig("m_qq_in", 16)
        m_x = sig("m_x_in", 16)
        conv = sig("conv_done")
        convact = sig("conv_silu", CT)
        zgate = sig("z_silu")
        chanT = sig("channels_psum", 2)
        tok = sig("tokens_ready")
        xwr = sig("xw_ready")
        ghr = sig("gh_ready", 2)
        cbps = sig("cb_psum")
        seg = sig("seg_psum", 2)
        decay = sig("decay_ready", 2)
        masked = sig("masked_ready", 2)
        yoff = sig("yoff_psum")
        stps = sig("state_psum")
        ydiag = sig("ydiag_psum")
        stdone = sig("state_done")
        gated = sig("gated")
        ssdrms = sig("ssd_root")
        ssdout = sig("ssd_out")
        logit = sig("index_psum", HEADS, SHORT)
        relu = sig("index_relu", HEADS, SHORT)
        scacc = sig("index_summed", HEADS, SHORT)
        sps = sig("scores_psum", HEADS)
        sread = sig("scores_read", HEADS)
        smax = sig("max_ready", HEADS)
        sexp = sig("probs_ready", HEADS)
        ptps = sig("probsT_psum", HEADS)
        ptc = sig("probsT_ready", HEADS)
        av = sig("av_psum", HEADS)
        mixr = sig("mix_ready")
        mixps = sig("mixT_psum")
        mixTr = sig("mixT_ready")
        outps = sig("out_psum")
        outrms = sig("out_root")
        x1r = sig("x1_ready")
        x1rms = sig("x1_root")
        h2r = sig("h2_ready")
        h2ps = sig("h2T_psum")
        h2Tr = sig("h2T_ready")
        pqps = sig("peer_q_psum")
        pqr = sig("peer_q_ready")
        pss = sig("sub_scores_psum")
        s2 = sig("sub_scores_ready", 2)
        fvr = sig("top_scores_ready")
        gexp = sig("gate_exp")
        prep = sig("experts_chosen")
        idxc = sig("indices_taken", 2)
        dot = sig("dot_done", SLOTS)
        gelu = sig("gelu_done", HEADS)
        wready = sig("weights_ready", HEADS)
        dg = sig("diag_ready", SLOTS)
        vused = sig("v_used", V_USED)
        frsum = sig("f_sumsq")
        frms = sig("f_root")
        xfin = sig("x_final")
        xcommit = sig("x1_taken")
        xout = sig("x_out", 16)
        u_in = [sem(f"u_in{r}") for r in range(UR)]
        v_in = [sem(f"v_in{r}") for r in range(VR)]
        vstep = sem("vector_steps")
        pstep = sem("vector_expert_steps")
        astep = sem("scalar_steps")
        bstep = sem("vector_setup_steps")
        rstep = sem("vector_projection_steps")

        s_room = sem("room_seen")
        s_turn = sem("turn_seen")

        FIRST, LOOP, FINAL = plan(PHASES, first=True), plan(PHASES), plan(LAST_PHASES)

        block = ctx.enter_context(nc.Block())

        @block.sync
        def _(sp):
            x_blocks = x.rearrange("o (b p) d -> b p (o d)", p=P)
            out_blocks = out.rearrange("o (b p) d -> b p (o d)", p=P)
            sp.dma_start(scT, c.rearrange("o (k p) -> p (o k)", p=P), allow_slow_non_contiguous=True).then_inc(s_rows, 16)
            sp.dma_start(pos_i, positions.rearrange("o (b p) -> p (o b)", p=P), allow_slow_non_contiguous=True).then_inc(s_rows, 16)
            sp.dma_start(b_row, b_ada[0:1, 0:3072]).then_inc(s_brow[0], 16)
            for n in range(2 * KC):
                half, k = n // KC, n % KC
                if n >= 3:
                    sp.wait_ge(s_adaused, n - 2)
                sp.dma_start(ada_buf[n % 3], w_ada[0, k * P:(k + 1) * P, half * 3072:(half + 1) * 3072])\
                    .then_inc(s_ada[n % 3], 16)
                if n == 3:
                    for dst, src in ((A1, pre_mix_g), (P1, post_mix_g), (A2, pre_ffn_g), (P2, post_ffn_g)):
                        sp.dma_start(dst, src[0, :].partition_broadcast(P)).then_inc(s_gain, 16)
                    sp.dma_start(ssdg, ssd_norm_g[0, :].partition_broadcast(P)).then_inc(s_gain, 16)
                if n == KC + 2:
                    sp.dma_start(b_row, b_ada[0:1, 3072:6144]).then_inc(s_brow[1], 16)
            for k in range(KC):
                sp.dma_start(w_in_sb[:, k, :], w_in[0, k * P:(k + 1) * P, :]).then_inc(s_win, 16)
            with sp.Fori(0, NB) as b:
                a_rot.wait(sp, b, 1)
                a_xbc.wait(sp, b, 1)
                sp.dma_start(spill[b], stag).then_inc(a_out.sem, 16)
            a_out.wait(sp, NB, 0)
            a_proj.wait(sp, NB, 0)

            def mix_loads(b):
                prep.wait(sp, b, 0)
                sp.dma_start(xc[:, :, 3:131], spill[b, :, 1536:2560].rearrange("p (a n) -> p a n", a=CT))\
                    .then_inc(m_xbc.sem, 16)
                sp.dma_start(zt, spill[b, :, 1024:1536]).then_inc(m_z.sem, 16)
                sp.dma_start(T[:, 0:1024], spill[b, :, 0:1024]).then_inc(m_qq.sem, 16)

            def x_load(b):
                xcommit.wait(sp, b, 0)
                sp.dma_start(x1n, x_blocks[b]).then_inc(m_x.sem, 16)

            def peer_store(b):
                xfin.wait(sp, b, 1)
                sp.dma_start(out_blocks[b], x1c).then_inc(xout.sem, 16)

            mix_loads(0)
            x_load(0)
            sp.dma_start(w_out_sb, w_out[0].rearrange("(k p) n -> p k n", p=P)).then_inc(s_wout, 16)
            sp.dma_start(w_q_sb, peer_w_q[0].rearrange("(k p) n -> p k n", p=P)).then_inc(s_wq, 16)
            mix_loads(1)
            x_load(1)
            with sp.Fori(1, NB - 1) as b:
                mix_loads(b + 1)
                xfin.wait(sp, b, 0)
                sp.dma_start(out_blocks[b - 1], x1c).then_inc(xout.sem, 16)
                x_load(b + 1)
            peer_store(NB - 2)
            peer_store(NB - 1)
            xout.wait(sp, NB, 0)

        @block.gpsimd
        def _(pool):
            n = 0

            def made(ins):
                nonlocal n
                n += 1
                ins.then_inc(s_conststep, 1)
                pool.wait_ge(s_conststep, n)

            made(pool.memset(ident, 0.0))
            made(pool.affine_select(out=ident, in_=ident, compare_op=ALU.not_equal, fill=1.0, base=0,
                                    pattern=[[-1, P]], channel_multiplier=1))
            made(pool.memset(ones, 1.0))
            made(pool.affine_select(out=upto, in_=ones, compare_op=ALU.is_ge, fill=0.0, base=0,
                                    pattern=[[1, P]], channel_multiplier=-1))
            made(pool.affine_select(out=after, in_=ones, compare_op=ALU.is_gt, fill=0.0, base=0,
                                    pattern=[[-1, P]], channel_multiplier=1))
            made(pool.memset(eps, EPS))
            made(pool.iota(iota_i, pattern=[[1, PK]], base=0, channel_multiplier=0))
            for i in range(HALF):
                made(pool.memset(inv_freq[:, i:i + 1], float(THETA ** (-2.0 * i / HD))))
            made(pool.memset(state, 0.0))
            made(pool.memset(hist.rearrange("p a n -> p (a n)"), 0.0))
            made(pool.memset(causal, 0.0))
            made(pool.affine_select(out=causal, in_=causal, compare_op=ALU.is_ge, fill=NEG, base=7 * P,
                                    pattern=[[-1, SEQ + 7 * P]], channel_multiplier=1))
            pool.sem_inc(s_consts, 1)
            pool.dma_start(convb, conv_b[0].rearrange("(c p) -> p c", p=P), allow_slow_non_contiguous=True).then_inc(s_small, 16)
            pool.dma_start(convw, conv_w[0].rearrange("j (c p) -> p (j c)", p=P),
                           allow_slow_non_contiguous=True).then_inc(s_small, 16)
            pool.dma_start(dtb, dt_bias[0, :].partition_broadcast(P)).then_inc(s_small, 16)
            pool.dma_start(neg_a, a_log[0, :].partition_broadcast(P)).then_inc(s_small, 16)
            pool.dma_start(dskip, d_skip[0, :].partition_broadcast(P)).then_inc(s_small, 16)
            pool.dma_start(keys_raw.rearrange("p h (t d) -> p h t d", t=2),
                           peer_sub_keys[0].rearrange("h t k d -> k h t d")).then_inc(s_keys, 16)
            x_blocks = x.rearrange("o (b p) d -> b p (o d)", p=P)
            for b in range(NB):
                if b:
                    pool.wait_ge(s_sumsq, b)
                pool.dma_start(x1n, x_blocks[b]).then_inc(s_xs, 16)
            pool.wait_ge(s_sumsq, NB)
            pool.dma_start(x1n, x_blocks[0]).then_inc(a_x.sem, 16)
            with pool.Fori(1, NB) as b:
                a_h.wait(pool, b, 0)
                pool.dma_start(x1n, x_blocks[b]).then_inc(a_x.sem, 16)

            def experts(b, steps):
                prep.wait(pool, b, 1)
                dot.wait(pool, b, 0)
                pool.sem_inc(s_room, 1)
                pool.tensor_copy(idxu, idxn).then_inc(idxc.sem, 1)
                idxc.wait(pool, b, 1)
                pool.sem_inc(s_room, 1)
                for kind, n, _ in steps:
                    if kind == "u":
                        r = n % UR
                        if n >= UR:
                            dot.wait(pool, b, n - UR + 1)
                            pool.sem_inc(s_room, 1)
                        pool.indirect_dma_start(
                            out=u_ring[r], out_offset=None, in_=peer_u[0],
                            in_offset=bass.IndirectOffsetOnAxis(ap=idxu[:, n:n + 1], axis=0),
                        ).then_inc(u_in[r], 16)
                    else:
                        back = SLOTS if kind == "w" else 0
                        if n == 0:
                            vused.wait(pool, b, 0)
                            pool.sem_inc(s_room, 1)
                            pool.tensor_copy(idxv, idxn).then_inc(idxc.sem, 1)
                            idxc.wait(pool, b, 2)
                            pool.sem_inc(s_room, 1)
                        r = n % VR
                        if n >= VR:
                            vused.wait(pool, b, n - VR + 1 - (V_USED if back else 0))
                            pool.sem_inc(s_room, 1)
                        pool.indirect_dma_start(
                            out=v_ring[r], out_offset=None, in_=peer_v[0],
                            in_offset=bass.IndirectOffsetOnAxis(ap=idxv[:, n:n + 1], axis=0),
                        ).then_inc(v_in[r], 16)

            experts(0, FIRST)
            with pool.Fori(1, NB - 1) as b:
                experts(b, LOOP)
            experts(NB - 1, FINAL)

        @block.scalar
        def _(act):
            steps = Steps(act, astep)
            sc = nc.scalar
            act.wait_ge(s_rows, 32)
            sc.activation(scT, scT, ACT.Silu).then_inc(s_silu, 1)
            act.wait_ge(s_consts, 1)
            for b in range(NB):
                act.wait_ge(s_xs, 16 * (b + 1))
                sc.activation(h2n, x1n, ACT.Square, accum_out=rowsum[:, b:b + 1]).then_inc(s_sumsq, 1)
            act.wait_ge(s_sumsq, NB)
            sc.activation(rstd, rowsum, ACT.Sqrt, scale=1.0 / D, bias=eps).then_inc(s_root, 1)
            act.wait_ge(s_small, 16 * 5)
            act.wait_ge(s_ang, 1)
            sc.activation(sinT, sinT, ACT.Sin)
            sc.activation(cosT, cosT, ACT.Sin).then_inc(s_trig, 1)

            def project(b):
                a_hps.wait(act, b, 1)
                sc.copy(hT.rearrange("p a n -> p (a n)"), bank(0, 2)).then_inc(a_hT.sem, 1)
                a_rope.wait(act, b, 0)
                a_out.wait(act, b, 0)
                a_proj.wait(act, b, 1)
                sc.copy(raw[:, 0:512], bank(2))
                a_proj.wait(act, b, 2)
                kk = bank(3)[:, 0:128].rearrange("p (g d) -> p g d", g=2)
                for twice in range(2):
                    sc.copy(raw[:, 1024:1280].rearrange("p (g t d) -> p g t d", g=2, t=2)[:, :, twice, :], kk)
                sc.copy(raw[:, 512:768], bank(3)[:, 256:512])
                sc.copy(vv[:, b, :], bank(3)[:, 128:256])
                a_proj.wait(act, b, 3)
                sc.copy(raw[:, 768:1024], bank(4)[:, 0:256])
                for twice in range(2):
                    last = sc.copy(raw[:, 1280 + 64 * twice:1344 + 64 * twice], bank(4)[:, 256:320])
                last.then_inc(a_raw.sem, 1)
                sc.copy(grid(dtwi, NB)[:, b, :], bank(4)[:, 320:336])
                a_proj.wait(act, b, 4)
                sc.copy(stag[:, 1024:1536], bank(5))
                a_rps.wait(act, b, 1)
                sc.copy(stag[:, 0:512], bank(0))
                sc.copy(stag[:, 512:1024], bank(1))
                for i, kT in enumerate((k0T, k1T, kiT)):
                    last = sc.copy(grid(kT, NB)[:, b, :], bank(2)[:, i * P:(i + 1) * P])
                last.then_inc(a_rot.sem, 1)

            project(0)
            with act.Fori(1, NB) as b:
                project(b)

            act.wait_ge(s_dtv, 1)
            sc.activation(small[:, 0:64], small[:, 0:64], ACT.Exp, scale=-1.0)
            sc.activation(neg_a, neg_a, ACT.Exp).then_inc(s_dta, 1)
            act.wait_ge(s_dtv, 2)
            sc.activation(small[:, 64:128], small[:, 64:128], ACT.Ln).then_inc(s_dta, 1)
            act.wait_ge(s_dtv, 4)
            sc.activation(eac, bank(0)[:, 0:64], ACT.Exp)
            sc.activation(etot, bank(0)[:, 64:128], ACT.Exp)
            sc.activation(dec, small[:, 0:64], ACT.Exp).then_inc(s_dta, 1)

            def root(col, width):
                return sc.activation(stat[:, col:col + 1], stat[:, col:col + 1], ACT.Sqrt,
                                     scale=1.0 / width, bias=eps)

            def mixing(b, nb):
                steps.begin()
                yield 8
                conv.wait(act, b, 1)
                for t in range(CT):
                    sc.activation(cv[:, t, :], cv[:, t, :], ACT.Silu, bias=convb[:, t:t + 1])\
                        .then_inc(convact.sem, 1)
                yield 10
                m_z.wait(act, b, 16)
                sc.activation(zt, zt, ACT.Silu).then_inc(zgate.sem, 1)
                for g in range(2):
                    yield 17 + 2 * g
                    seg.wait(act, b, g + 1)
                    sc.activation(L[:, g * 512:(g + 1) * 512], bank(2 + g), ACT.Exp).then_inc(decay.sem, 1)
                yield 27
                gated.wait(act, b, 1)
                steps(sc.activation(ytmp, yy, ACT.Square, accum_out=stat[:, 0:1]))
                root(0, 512).then_inc(ssdrms.sem, 1)
                nk = nb * P
                yield 28
                ssdout.wait(act, b, 1)
                for h in range(HEADS if nb > SHORT else 0):
                    yield 29 + h
                    if h >= 2:
                        scacc.wait(act, b, h - 1)
                    logit.wait(act, b, h + 1)
                    sc.activation(RL[h % 2][:, 0:nk], (SB if h % 2 == 0 else TB)[:, 0:nk], ACT.Relu, scale=HD ** -0.5)\
                        .then_inc(relu.sem, 1)
                for h in range(HEADS + 1):
                    if h < HEADS:
                        yield 118 + 3 * h
                        smax.wait(act, b, h + 1)
                        sc.activation(RL[h % 2][:, 0:nk], RL[h % 2][:, 0:nk], ACT.Exp, bias=negmax[:, h:h + 1],
                                      accum_out=psums[:, h:h + 1]).then_inc(sexp.sem, 1)
                    yield 119 + 3 * h
                    if h < HEADS:
                        ptps.wait(act, b, h + 1)
                        if h:
                            av.wait(act, b, h)
                        sc.copy(PT.rearrange("p a n -> p (a n)")[:, 0:nk], TB[:, 0:nk]).then_inc(ptc.sem, 1)
                yield 148
                outps.wait(act, b, 1)
                steps(sc.activation(otmp, SB, ACT.Square, accum_out=stat[:, 1:2]))
                root(1, D).then_inc(outrms.sem, 1)
                yield 151
                x1r.wait(act, b, 1)
                steps(sc.activation(otmp, x1n, ACT.Square, accum_out=stat[:, 2:3]))
                root(2, D).then_inc(x1rms.sem, 1)
                yield 160
                pqps.wait(act, b, 1)
                sc.copy(qpT.rearrange("p a n -> p (a n)"), SB).then_inc(pqr.sem, 1)
                yield 161
                pss.wait(act, b, 1)
                sc.copy(ss[:, 0:1024], SB).then_inc(s2.sem, 1)
                sc.copy(ss[:, 1024:2048], TB).then_inc(s2.sem, 1)
                yield 196
                fvr.wait(act, b, 1)
                sc.activation(gn, gn, ACT.Exp).then_inc(gexp.sem, 1)

            def finish(b, back):
                vused.wait(act, b, V_USED - back * V_USED)
                sc.activation(PT.rearrange("p a n -> p (a n)"), VB, ACT.Square, accum_out=stat[:, 3:4])\
                    .then_inc(frsum.sem, 1)
                frsum.wait(act, b, 1 - back)
                root(3, D).then_inc(frms.sem, 1)

            def experts(b, plan_steps, weave):
                at = moments(plan_steps)
                for i in range(len(plan_steps)):
                    kind, n, stage = plan_steps[i]
                    for what, h in at.get(i, ()):
                        if what == "gelu":
                            s = slice(h * PK, (h + 1) * PK)
                            dot.wait(act, b, (h + 1) * PK)
                            sc.activation(gel[:, s], dots[:, s], ACT.Gelu).then_inc(gelu.sem, 1)
                        if what == "sum" and plan_steps is not FIRST:
                            finish(b, 1)
                    if kind != "u":
                        back = SLOTS if kind == "w" else 0
                        if kind == "v":
                            wready.wait(act, b, n // PK + 1)
                        if n >= GR or kind == "w":
                            vused.wait(act, b, n - GR + 1 - (V_USED if back else 0))
                        sc.activation(diag[n % GR], ident, ACT.Copy, scale=wgt[:, n:n + 1]).then_inc(dg.sem, 1)
                    weave.upto(stage)
                weave.upto(END - 1)
                wready.wait(act, b, HEADS)

            Weave(mixing(0, 1)).upto(END - 1)
            experts(0, FIRST, Weave(mixing(1, 2)))
            with act.Fori(1, NB // 2 - 1) as b:
                experts(b, LOOP, Weave(mixing(b + 1, NB // 2)))
            with act.Fori(NB // 2 - 1, NB - 1) as b:
                experts(b, LOOP, Weave(mixing(b + 1, NB)))
            experts(NB - 1, FINAL, Weave(iter(())))
            finish(NB - 1, 0)

        @block.tensor
        def _(pe):
            te = nc.tensor

            def turn(dst, src, tiles):
                for i in range(tiles):
                    last = te.transpose(dst[:, i * P:(i + 1) * P], src[:, i * P:(i + 1) * P], ident)
                return last

            def turn_rows(dst, src, tiles):
                for i in range(tiles):
                    last = te.transpose(dst[:, i * P:(i + 1) * P], src[:, i, :], ident)
                return last

            pe.wait_ge(s_consts, 1)
            pe.wait_ge(s_wide, 1)
            wide = grid(mix, KC)
            for half in range(2):
                pe.wait_ge(s_brow[half], 16)
                if half:
                    pe.wait_ge(s_mod, 1)
                for j in range(6):
                    te.matmul(bank(j), ones[0:1, :], b_row[:, j * 512:(j + 1) * 512], start=True, stop=False)
                for k in range(KC):
                    n = half * KC + k
                    pe.wait_ge(s_ada[n % 3], 16 * (n // 3 + 1))
                    for j in range(6):
                        last = te.matmul(bank(j), wide[:, k, :], ada_buf[n % 3][:, j * 512:(j + 1) * 512],
                                         start=False, stop=(k == KC - 1))
                    last.then_inc(s_adaused, 1)
            pe.wait_ge(s_keys, 16)
            pe.wait_ge(s_mod, 2)
            turn_rows(bank(0, 2), keys_raw, HEADS).then_inc(s_keyps, 1)
            pe.wait_ge(s_keysT, 1)
            pe.wait_ge(s_win, 16 * KC)

            def project(b):
                a_rot.wait(pe, b, 0)
                a_h.wait(pe, b, 1)
                turn(bank(0, 2), h2n, KC).then_inc(a_hps.sem, 1)
                a_hT.wait(pe, b, 1)
                groups = [((2, 0, 512, 0),), ((3, 0, 512, 512),), ((4, 0, C_Z - 1024, 1024), (4, C_Z - 1024, 8, C_DT)),
                          ((5, 0, 512, C_Z),)]
                for parts in groups:
                    for i, at, width, col in parts:
                        for k in range(KC):
                            last = te.matmul(bank(i)[:, at:at + width], hT[:, k, :], w_in_sb[:, k, col:col + width],
                                             start=(k == 0), stop=(k == KC - 1))
                    last.then_inc(a_proj.sem, 1)
                a_xbc.wait(pe, b, 0)
                for t in range(CT):
                    for k in range(KC):
                        last = te.matmul(bank(6 + t // 4)[:, t % 4 * P:(t % 4 + 1) * P],
                                         w_in_sb[:, k, C_XBC + t * P:C_XBC + (t + 1) * P], hT[:, k, :],
                                         start=(k == 0), stop=(k == KC - 1))
                    if t % 4 == 3:
                        last.then_inc(a_proj.sem, 1)
                a_rope.wait(pe, b, 1)
                a_raw.wait(pe, b, 1)
                turn(bank(0, 2), rot, 8)
                turn(bank(2), rot[:, 1024:1408], 3).then_inc(a_rps.sem, 1)

            project(0)
            with pe.Fori(1, NB) as b:
                project(b)

            a_rot.wait(pe, NB, 0)
            pe.wait_ge(s_dtv, 3)
            te.matmul(bank(0)[:, 0:64], upto, adt, start=True, stop=True)
            te.matmul(bank(0)[:, 64:128], ones, adt, start=True, stop=True).then_inc(s_dtp, 1)

            def mixing(b, nb):
                yield 10
                convact.wait(pe, b, CT)
                for t in range(4):
                    last = te.transpose(XB[:, t * P:(t + 1) * P], cv[:, t, :], ident)
                last.then_inc(chanT.sem, 1)
                for t in range(2):
                    last = te.transpose(OB[:, t * P:(t + 1) * P], cv[:, 4 + t, :], ident)
                last.then_inc(chanT.sem, 1)
                for g in range(2):
                    last = te.matmul(bank(4)[:, g * P:(g + 1) * P], cv[:, 4 + g, :], cv[:, 6 + g, :],
                                     start=True, stop=True)
                last.then_inc(cbps.sem, 1)
                for g in range(2):
                    yield 16 + 2 * g
                    ghr.wait(pe, b, g + 1)
                    for i in range(4):
                        last = te.matmul(bank(2 + g)[:, i * P:(i + 1) * P], gh[:, i, :], upto, start=True, stop=True)
                    last.then_inc(seg.sem, 1)
                yield 18
                tok.wait(pe, b, 1)
                stdone.wait(pe, b, 0)
                for g in range(2):
                    last = te.matmul(OB[:, g * 256:(g + 1) * 256], cv[:, 6 + g, :], state[:, g * 256:(g + 1) * 256],
                                     start=True, stop=True)
                last.then_inc(yoff.sem, 1)
                xwr.wait(pe, b, 1)
                for g in range(2):
                    last = te.matmul(XB[:, g * 256:(g + 1) * 256], btok[:, g * P:(g + 1) * P],
                                     xw[:, g * 256:(g + 1) * 256], start=True, stop=True)
                last.then_inc(stps.sem, 1)
                for g in range(2):
                    yield 21 + 2 * g
                    masked.wait(pe, b, g + 1)
                    for h in range(4 * g, 4 * g + 4):
                        last = te.matmul(bank(5)[:, h * HD:(h + 1) * HD], L[:, h * P:(h + 1) * P],
                                         xdt[:, h * HD:(h + 1) * HD], start=True, stop=True)
                last.then_inc(ydiag.sem, 1)
                m_qq.wait(pe, b, 16)
                nk = nb * P
                wide_steps = [slice(at, min(at + 512, nk)) for at in range(0, nk, 512)]
                yield 28
                gated.wait(pe, b, 1)
                for h in range(HEADS if nb > SHORT else 0):
                    yield 28 + h
                    if h >= 2:
                        relu.wait(pe, b, h - 1)
                    dst = SB if h % 2 == 0 else TB
                    half = slice(h % 2 * HD, h % 2 * HD + HD)
                    for part in wide_steps:
                        last = te.matmul(dst[:, part], qiT[half, h // 2, :], kiT[half, part], start=True, stop=True)
                    last.then_inc(logit.sem, 1)

                def scores(h):
                    if h:
                        sread.wait(pe, b, h)
                    elif nb > SHORT:
                        relu.wait(pe, b, HEADS)
                    half = slice(h % 2 * HD, h % 2 * HD + HD)
                    kT = (k0T, k1T)[h // 4]
                    for part in wide_steps:
                        last = te.matmul(SB[:, part], qT[half, h // 2, :], kT[half, part], start=True, stop=True)
                    last.then_inc(sps.sem, 1)

                def values(h):
                    ptc.wait(pe, b, h + 1)
                    for j in range(nb):
                        last = te.matmul(OB[:, h * HD:(h + 1) * HD], PT[:, j, :],
                                         vv[:, j, h // 4 * HD:(h // 4 + 1) * HD], start=(j == 0), stop=(j == nb - 1))
                    last.then_inc(av.sem, 1)

                yield 110
                scores(0)
                for h in range(HEADS):
                    yield 118 + 3 * h
                    if h < HEADS - 1:
                        scores(h + 1)
                    sexp.wait(pe, b, h + 1)
                    if h:
                        ptc.wait(pe, b, h)
                    turn(TB, RL[h % 2], nb).then_inc(ptps.sem, 1)
                    if h:
                        yield 119 + 3 * h
                        values(h - 1)
                yield 142
                values(HEADS - 1)
                yield 144
                mixr.wait(pe, b, 1)
                turn(TB, mix, KC).then_inc(mixps.sem, 1)
                for j in range(2):
                    if j == 0:
                        yield 145
                        mixTr.wait(pe, b, 1)
                        pe.wait_ge(s_wout, 16)
                    for k in range(KC):
                        yield 145 + (j * KC + k) / 5
                        last = te.matmul(SB[:, j * 512:(j + 1) * 512], mixT[:, k, :],
                                         w_out_sb[:, k, j * 512:(j + 1) * 512], start=(k == 0), stop=(k == KC - 1))
                last.then_inc(outps.sem, 1)
                yield 155
                h2r.wait(pe, b, 1)
                turn(TB, h2n, KC).then_inc(h2ps.sem, 1)
                yield 156
                h2Tr.wait(pe, b, 1)
                pe.wait_ge(s_wq, 16)
                for h in range(HEADS):
                    yield 156 + h / 2
                    for k in range(KC):
                        last = te.matmul(SB[:, h * P:(h + 1) * P], w_q_sb[:, k, h * P:(h + 1) * P], h2T[:, k, :],
                                         start=(k == 0), stop=(k == KC - 1))
                last.then_inc(pqps.sem, 1)
                yield 160
                pqr.wait(pe, b, 1)
                for i in range(LISTS):
                    half = slice(i // HEADS * HD, i // HEADS * HD + HD)
                    last = te.matmul(bank(2 + i // 4)[:, i % 4 * P:(i % 4 + 1) * P], qpT[half, i % HEADS, :],
                                     keysT[half, i % HEADS, :], start=True, stop=True)
                last.then_inc(pss.sem, 1)

            def experts(b, plan_steps, weave):
                for kind, n, stage in plan_steps:
                    if kind != "u":
                        back = SLOTS if kind == "w" else 0
                        r = n % VR
                        if n == 0:
                            xfin.wait(pe, b, 0)
                        dg.wait(pe, b, n + 1 - back)
                        pe.wait_ge(v_in[r], 16 * (b * uses(VR, r) + n // VR + 1 - back // VR))
                        for j in range(2):
                            last = te.matmul(VB[:, j * 512:(j + 1) * 512], diag[n % GR],
                                             v_ring[r][:, j * 512:(j + 1) * 512], start=(n == 0), stop=(n == SLOTS - 1))
                        last.then_inc(vused.sem, 2 if n == SLOTS - 1 else 1)
                    weave.upto(stage)
                weave.upto(END - 1)

            Weave(mixing(0, 1)).upto(END - 1)
            experts(0, FIRST, Weave(mixing(1, 2)))
            with pe.Fori(1, NB // 2 - 1) as b:
                experts(b, LOOP, Weave(mixing(b + 1, NB // 2)))
            with pe.Fori(NB // 2 - 1, NB - 1) as b:
                experts(b, LOOP, Weave(mixing(b + 1, NB)))
            experts(NB - 1, FINAL, Weave(iter(())))

        @block.vector
        def _(vec):
            ve = nc.vector
            setup = Steps(vec, bstep)
            steps = Steps(vec, vstep)
            pert = Steps(vec, pstep)
            ropes = Steps(vec, rstep)

            vec.wait_ge(s_silu, 1)
            ve.tensor_copy(grid(mix, KC), over_last(scT, P)).then_inc(s_wide, 1)
            vec.wait_ge(s_consts, 1)
            vec.wait_ge(s_rows, 32)
            setup(ve.tensor_copy(iota16, iota_i))
            setup(ve.tensor_copy(pos_f, pos_i))
            setup(ve.tensor_tensor(grid(ang, NB), over_last(pos_f, HALF), over_first(inv_freq, NB), ALU.mult))
            RND = 12582912.0
            C1 = 6.28125
            C2 = float(2 * math.pi - 6.28125)
            PI = 3.1415925
            setup(ve.tensor_scalar(ang2, ang, 1.0 / (2 * math.pi), RND, ALU.mult, ALU.add))
            setup(ve.tensor_scalar(ang2, ang2, -RND, None, ALU.add))
            setup(ve.scalar_tensor_tensor(out=ang, in0=ang2, scalar=-C1, in1=ang, op0=ALU.mult, op1=ALU.add))
            setup(ve.scalar_tensor_tensor(out=ang, in0=ang2, scalar=-C2, in1=ang, op0=ALU.mult, op1=ALU.add))
            setup(ve.tensor_scalar(sinT, ang, PI, -PI, ALU.min, ALU.max))
            setup(ve.tensor_scalar(ang, ang, math.pi / 2, None, ALU.add))
            setup(ve.tensor_scalar(ang2, ang, math.pi, -2 * math.pi, ALU.is_gt, ALU.mult))
            setup(ve.tensor_tensor(ang, ang, ang2, ALU.add))
            ve.tensor_scalar(cosT, ang, PI, -PI, ALU.min, ALU.max).then_inc(s_ang, 1)
            vec.wait_ge(s_root, 1)
            setup(ve.reciprocal(rstd, rstd))
            vec.wait_ge(s_small, 16 * 5)
            vec.wait_ge(s_gain, 16 * 5)
            vec.wait_ge(s_adaused, KC)
            ve.tensor_copy(B1, bank(0, 2))
            ve.scalar_tensor_tensor(out=A1, in0=bank(2, 2), scalar=1.0, in1=A1, op0=ALU.add, op1=ALU.mult)
            ve.tensor_tensor(P1, bank(4, 2), P1, ALU.mult).then_inc(s_mod, 1)
            vec.wait_ge(s_adaused, 2 * KC)
            ve.tensor_copy(B2, bank(0, 2))
            ve.scalar_tensor_tensor(out=A2, in0=bank(2, 2), scalar=1.0, in1=A2, op0=ALU.add, op1=ALU.mult)
            ve.tensor_tensor(P2, bank(4, 2), P2, ALU.mult).then_inc(s_mod, 1)
            vec.wait_ge(s_mod, 2)
            vec.wait_ge(s_keyps, 1)
            ve.tensor_copy(keysT.rearrange("p a n -> p (a n)"), bank(0, 2)).then_inc(s_keysT, 1)
            vec.wait_ge(s_trig, 1)

            heads = 22
            def project(b):
                ropes.begin()
                a_x.wait(vec, b, 16)
                a_hps.wait(vec, b, 0)
                ropes(ve.scalar_tensor_tensor(out=h2n, in0=x1n, scalar=rstd[:, bass.ds(b, 1)], in1=A1,
                                              op0=ALU.mult, op1=ALU.mult))
                ve.tensor_tensor(h2n, h2n, B1, ALU.add).then_inc(a_h.sem, 1)
                a_raw.wait(vec, b, 1)
                a_rps.wait(vec, b, 0)
                r3, o3, t3 = grid(raw, heads), grid(rot, heads), grid(rtmp, heads)
                cos = over_first(grid(cosT, NB)[:, b, :], heads)
                sin = over_first(grid(sinT, NB)[:, b, :], heads)
                x1, x2 = r3[:, :, 0:HALF], r3[:, :, HALF:HD]
                ropes(ve.tensor_tensor(t3, x2, sin, ALU.mult))
                ropes(ve.tensor_tensor(o3[:, :, 0:HALF], x1, cos, ALU.mult))
                ropes(ve.tensor_tensor(o3[:, :, 0:HALF], o3[:, :, 0:HALF], t3, ALU.subtract))
                ropes(ve.tensor_tensor(t3, x1, sin, ALU.mult))
                ropes(ve.tensor_tensor(o3[:, :, HALF:HD], x2, cos, ALU.mult))
                ve.tensor_tensor(o3[:, :, HALF:HD], o3[:, :, HALF:HD], t3, ALU.add).then_inc(a_rope.sem, 1)
                a_proj.wait(vec, b, 6)
                a_out.wait(vec, b, 0)
                ve.tensor_copy(stag[:, 1536:2560], bank(6, 2)).then_inc(a_xbc.sem, 1)

            project(0)
            with vec.Fori(1, NB) as b:
                project(b)

            small3 = [small[:, i * 64:(i + 1) * 64] for i in range(6)]
            a_rot.wait(vec, NB, 0)
            dw = grid(dtwi, NB)
            setup(ve.tensor_scalar(grid(wis, NB), dw[:, :, 0:8], float(HEADS ** -0.5), None, ALU.mult))
            setup(ve.tensor_tensor(grid(small3[2], NB), dw[:, :, 8:16], over_first(dtb, NB), ALU.add))
            setup(ve.tensor_scalar(small3[3], small3[2], 0.0, None, ALU.max))
            setup(ve.tensor_scalar(small3[4], small3[2], -1.0, None, ALU.mult))
            ve.tensor_tensor(small3[0], small3[2], small3[4], ALU.max).then_inc(s_dtv, 1)
            vec.wait_ge(s_dta, 1)
            setup(ve.tensor_scalar(neg_a, neg_a, -1.0, None, ALU.mult))
            setup(ve.tensor_scalar(small3[1], small3[0], 1.0, None, ALU.add))
            setup(ve.tensor_scalar(small3[2], small3[1], -1.0, None, ALU.add))
            setup(ve.tensor_scalar(small3[4], small3[2], 1e-30, None, ALU.max))
            setup(ve.reciprocal(small3[4], small3[4]))
            ve.tensor_tensor(small3[4], small3[4], small3[0], ALU.mult).then_inc(s_dtv, 1)
            vec.wait_ge(s_dta, 2)
            setup(ve.tensor_tensor(small3[4], small3[4], small3[1], ALU.mult))
            setup(ve.scalar_tensor_tensor(out=small3[5], in0=small3[2], scalar=0.0, in1=small3[0],
                                          op0=ALU.is_equal, op1=ALU.mult))
            setup(ve.tensor_tensor(small3[4], small3[4], small3[5], ALU.add))
            setup(ve.tensor_tensor(dt_s, small3[4], small3[3], ALU.add))
            ve.tensor_tensor(grid(adt, NB), grid(dt_s, NB), over_first(neg_a, NB), ALU.mult).then_inc(s_dtv, 1)
            vec.wait_ge(s_dtp, 1)
            setup(ve.tensor_copy(small3[0], bank(0)[:, 64:128]))
            ve.tensor_tensor(small3[0], small3[0], bank(0)[:, 0:64], ALU.subtract).then_inc(s_dtv, 1)
            vec.wait_ge(s_dta, 3)

            def mixing(b, nb):
                steps.begin()
                yield 0
                m_xbc.wait(vec, b, 16)
                steps(ve.tensor_copy(xc[:, :, 0:3], hist))
                w3 = grid(convw, TAPS)
                steps(ve.tensor_tensor(cv, xc[:, :, 3:131], over_last(w3[:, 3, :], P), ALU.mult))
                for j in range(3):
                    yield 2 + 2 * j
                    steps(ve.tensor_tensor(ctmp, xc[:, :, j:j + P], over_last(w3[:, j, :], P),
                                           ALU.mult))
                    yield 3 + 2 * j
                    if j < 2:
                        steps(ve.tensor_tensor(cv, cv, ctmp, ALU.add))
                    else:
                        ve.tensor_tensor(cv, cv, ctmp, ALU.add).then_inc(conv.sem, 1)
                steps(ve.tensor_copy(hist, xc[:, :, 128:131]))
                adt_b, dt_b = grid(adt, NB)[:, b, :], grid(dt_s, NB)[:, b, :]
                yield 9
                ve.tensor_tensor(gh, over_first(after, 4), over_last(adt_b[:, 0:4], P), ALU.mult)\
                    .then_inc(ghr.sem, 1)
                yield 12
                chanT.wait(vec, b, 2)
                steps(ve.tensor_copy(xtok, XB))
                steps(ve.tensor_tensor(grid(xdt, HEADS), grid(XB, HEADS), over_last(dt_b, HD), ALU.mult))
                ve.tensor_copy(btok, OB[:, 0:256]).then_inc(tok.sem, 1)
                yield 14
                ve.tensor_tensor(grid(xw, HEADS), grid(xdt, HEADS), over_last(grid(dec, NB)[:, b, :], HD),
                                 ALU.mult).then_inc(xwr.sem, 1)
                cbps.wait(vec, b, 1)
                steps(ve.tensor_tensor(cbm, bank(4)[:, 0:256].rearrange("p (g n) -> p g n", g=2),
                                       over_first(upto, 2), ALU.mult))
                yield 17
                seg.wait(vec, b, 1)
                ve.tensor_tensor(gh, over_first(after, 4), over_last(adt_b[:, 4:8], P), ALU.mult)\
                    .then_inc(ghr.sem, 1)
                for g in range(2):
                    yield 19 + 2 * g
                    decay.wait(vec, b, g + 1)
                    lg = grid(L[:, g * 512:(g + 1) * 512], 4)
                    ve.tensor_tensor(lg, lg, over_first(cbm[:, g, :], 4), ALU.mult).then_inc(masked.sem, 1)
                yield 23
                yoff.wait(vec, b, 1)
                steps(ve.tensor_tensor(grid(yy, HEADS), grid(OB, HEADS), over_last(grid(eac, NB)[:, b, :], HD),
                                       ALU.mult))
                steps(ve.tensor_tensor(grid(state, HEADS), grid(state, HEADS),
                                       over_last(grid(etot, NB)[:, b, :], HD), ALU.mult))
                stps.wait(vec, b, 1)
                ve.tensor_tensor(state, state, XB, ALU.add).then_inc(stdone.sem, 1)
                yield 25
                ydiag.wait(vec, b, 1)
                steps(ve.tensor_tensor(yy, yy, bank(5), ALU.add))
                steps(ve.tensor_tensor(grid(ytmp, HEADS), grid(xtok, HEADS), over_last(dskip, HD), ALU.mult))
                steps(ve.tensor_tensor(yy, yy, ytmp, ALU.add))
                zgate.wait(vec, b, 1)
                ve.tensor_tensor(yy, yy, zt, ALU.mult).then_inc(gated.sem, 1)
                yield 28
                ssdrms.wait(vec, b, 1)
                steps(ve.reciprocal(stat[:, 0:1], stat[:, 0:1]))
                ve.scalar_tensor_tensor(out=mix[:, 512:1024], in0=yy, scalar=stat[:, 0:1], in1=ssdg,
                                        op0=ALU.mult, op1=ALU.mult).then_inc(ssdout.sem, 1)
                wb = grid(wis, NB)[:, b, :]
                nk = nb * P
                scores, unseen = SC[:, 0:nk], AM[:, 0:nk]
                if nb > SHORT:
                    for h in range(HEADS):
                        yield 30 + h
                        relu.wait(vec, b, h + 1)
                        if h == 0:
                            ve.tensor_scalar(scores, RL[0][:, 0:nk], wb[:, 0:1], None, ALU.mult)\
                                .then_inc(scacc.sem, 1)
                        else:
                            scacc.wait(vec, b, h)
                            ve.scalar_tensor_tensor(out=scores, in0=RL[h % 2][:, 0:nk], scalar=wb[:, h:h + 1],
                                                    in1=scores, op0=ALU.mult, op1=ALU.add).then_inc(scacc.sem, 1)
                    yield 38
                    scacc.wait(vec, b, HEADS)
                    vec.sem_inc(s_turn, 1)
                    mask = causal[:, bass.ds((NB - 1 - b) * P, nk)]
                    steps(ve.tensor_tensor(scores, scores, mask, ALU.add))
                    for i in range(TOPK // 8):
                        yield 39 + i * 74 / 32
                        steps(ve.max(mx8, scores))
                        yield 40 + i * 74 / 32
                        steps(ve.match_replace(scores, mx8, scores, TAKEN))
                    yield 113
                    steps(ve.tensor_scalar(unseen, scores, LOW, NEG, ALU.is_gt, ALU.mult))
                    yield 115
                    steps(ve.tensor_tensor(unseen, unseen, mask, ALU.add))
                else:
                    steps(ve.tensor_copy(unseen, causal[:, (NB - 1 - b) * P:(NB - 1 - b) * P + nk]))
                for h in range(HEADS):
                    yield 116 + 3 * h
                    sps.wait(vec, b, h + 1)
                    if h >= 2:
                        ptps.wait(vec, b, h - 1)
                    ve.scalar_tensor_tensor(out=RL[h % 2][:, 0:nk], in0=SB[:, 0:nk], scalar=HD ** -0.5, in1=unseen,
                                            op0=ALU.mult, op1=ALU.add).then_inc(sread.sem, 1)
                    yield 117 + 3 * h
                    sread.wait(vec, b, h + 1)
                    ve.tensor_reduce(negmax[:, h:h + 1], RL[h % 2][:, 0:nk], AX.X, ALU.max, negate=True)\
                        .then_inc(smax.sem, 1)
                yield 143
                av.wait(vec, b, HEADS)
                steps(ve.reciprocal(rsums, psums))
                ve.tensor_tensor(grid(mix[:, 0:512], HEADS), grid(OB, HEADS), over_last(rsums, HD), ALU.mult)\
                    .then_inc(mixr.sem, 1)
                yield 145
                mixps.wait(vec, b, 1)
                ve.tensor_copy(mixT.rearrange("p a n -> p (a n)"), TB).then_inc(mixTr.sem, 1)
                yield 149
                outrms.wait(vec, b, 1)
                m_x.wait(vec, b, 16)
                steps(ve.reciprocal(stat[:, 1:2], stat[:, 1:2]))
                steps(ve.scalar_tensor_tensor(out=otmp, in0=SB, scalar=stat[:, 1:2], in1=P1,
                                              op0=ALU.mult, op1=ALU.mult))
                yield 150
                ve.tensor_tensor(x1n, x1n, otmp, ALU.add).then_inc(x1r.sem, 1)
                yield 152
                x1rms.wait(vec, b, 1)
                steps(ve.reciprocal(stat[:, 2:3], stat[:, 2:3]))
                steps(ve.scalar_tensor_tensor(out=h2n, in0=x1n, scalar=stat[:, 2:3], in1=A2,
                                              op0=ALU.mult, op1=ALU.mult))
                yield 154
                ve.tensor_tensor(h2n, h2n, B2, ALU.add).then_inc(h2r.sem, 1)
                yield 156
                h2ps.wait(vec, b, 1)
                ve.tensor_copy(h2T.rearrange("p a n -> p (a n)"), TB).then_inc(h2Tr.sem, 1)
                for i in range(LISTS):
                    yield 162 + i
                    if i % 8 == 0:
                        s2.wait(vec, b, i // 8 + 1)
                        vec.sem_inc(s_turn, 1)
                    s = ss[:, i * P:(i + 1) * P]
                    lo, hi = slice(i * PK, i * PK + 8), slice(i * PK + 8, (i + 1) * PK)
                    steps(ve.max(sv[:, lo], s))
                    steps(ve.max_index(si[:, lo], sv[:, lo], s))
                    steps(ve.match_replace(s, sv[:, lo], s, TAKEN))
                    steps(ve.max(sv[:, hi], s))
                    steps(ve.max_index(si[:, hi], sv[:, hi], s))
                yield 178
                steps(ve.tensor_copy(sif, si))
                sv4 = sv.rearrange("p (t h k) -> p t h k", h=HEADS, t=2)
                cand4 = cand.rearrange("p (h i j) -> p h i j", h=HEADS, i=PK)
                for h in range(HEADS):
                    steps(ve.tensor_tensor(cand4[:, h], over_last(sv4[:, 0, h], PK), over_first(sv4[:, 1, h], PK),
                                           ALU.add))
                for h in range(HEADS):
                    yield 181 + 2 * h
                    cd = cand[:, h * 256:(h + 1) * 256]
                    lo, hi = slice(h * PK, h * PK + 8), slice(h * PK + 8, (h + 1) * PK)
                    steps(ve.max(fv[:, lo], cd))
                    steps(ve.max_index(fp[:, lo], fv[:, lo], cd))
                    steps(ve.match_replace(cd, fv[:, lo], cd, TAKEN))
                    steps(ve.max(fv[:, hi], cd))
                    steps(ve.max_index(fp[:, hi], fv[:, hi], cd))
                yield 195
                steps(ve.tensor_reduce(gsum, grid(fv, HEADS), AX.X, ALU.max))
                ve.tensor_tensor(grid(gn, HEADS), grid(fv, HEADS), over_last(gsum, PK), ALU.subtract)\
                    .then_inc(fvr.sem, 1)
                idxc.wait(vec, b, 0)
                hot3 = hot.rearrange("p (n k) -> p n k", k=PK)
                for t in range(2):
                    yield 197 + 4 * t
                    if t == 0:
                        steps(ve.tensor_scalar(fpi, fp, 4, None, ALU.logical_shift_right))
                    else:
                        steps(ve.tensor_scalar(fpi, fp, 15, None, ALU.bitwise_and))
                    steps(ve.tensor_copy(fpf, fpi))
                    steps(ve.tensor_tensor(hot3, over_first(iota16, SLOTS), over_last(fpf, PK), ALU.is_equal))
                    yield 199 + 4 * t
                    sif4 = sif.rearrange("p (t h k) -> p t h k", h=HEADS, t=2)
                    for h in range(HEADS):
                        hh = hot3[:, h * PK:(h + 1) * PK, :]
                        steps(ve.tensor_tensor(hh, hh, over_first(sif4[:, t, h], PK), ALU.mult))
                    steps(ve.tensor_reduce((e1, fpf)[t], hot3, AX.X, ALU.add))
                steps(ve.scalar_tensor_tensor(out=e1, in0=e1, scalar=float(EXPERT_KEYS), in1=fpf,
                                              op0=ALU.mult, op1=ALU.add))
                steps(ve.tensor_copy(idxn, e1))
                gexp.wait(vec, b, 1)
                steps(ve.tensor_reduce(gsum, grid(gn, HEADS), AX.X, ALU.add))
                steps(ve.reciprocal(gsum, gsum))
                ve.tensor_tensor(grid(gn, HEADS), grid(gn, HEADS), over_last(gsum, PK), ALU.mult)\
                    .then_inc(prep.sem, 1)

            def finish(b, back):
                xcommit.wait(vec, b, 1 - back)
                frms.wait(vec, b, 1 - back)
                pert(ve.reciprocal(stat[:, 3:4], stat[:, 3:4]))
                pert(ve.scalar_tensor_tensor(out=VB, in0=VB, scalar=stat[:, 3:4], in1=P2,
                                             op0=ALU.mult, op1=ALU.mult))
                ve.tensor_tensor(x1c, x1c, VB, ALU.add).then_inc(xfin.sem, 1)

            def experts(b, plan_steps, weave):
                at = moments(plan_steps)
                pert.begin()
                prep.wait(vec, b, 1)
                dot.wait(vec, b, 0)
                wready.wait(vec, b, 0)
                ve.tensor_copy(gc, gn)
                pert(ve.tensor_copy(h2c, h2n))
                for i in range(max(max(at) + 1, len(plan_steps))):
                    for what, h in at.get(i, ()):
                        if what == "weights":
                            s = slice(h * PK, (h + 1) * PK)
                            gelu.wait(vec, b, h + 1)
                            if plan_steps is not FIRST:
                                dg.wait(vec, b, (h + 1) * PK - SLOTS)
                            ve.tensor_tensor(wgt[:, s], gel[:, s], gc[:, s], ALU.mult).then_inc(wready.sem, 1)
                        if what == "finish" and plan_steps is not FIRST:
                            finish(b, 1)
                        if what == "commit":
                            xout.wait(vec, b, 0)
                            ve.tensor_copy(x1c, x1n).then_inc(xcommit.sem, 1)
                    if i >= len(plan_steps):
                        continue
                    kind, n, stage = plan_steps[i]
                    if kind == "u":
                        r = n % UR
                        vec.wait_ge(u_in[r], 16 * (b * uses(UR, r) + n // UR + 1))
                        ve.tensor_tensor_reduce(u_ring[r], u_ring[r], h2c, 1.0, 0.0, ALU.mult, ALU.add,
                                                dots[:, n:n + 1]).then_inc(dot.sem, 1)
                    weave.upto(stage)
                weave.upto(END - 1)

            Weave(mixing(0, 1)).upto(END - 1)
            experts(0, FIRST, Weave(mixing(1, 2)))
            with vec.Fori(1, NB // 2 - 1) as b:
                experts(b, LOOP, Weave(mixing(b + 1, NB // 2)))
            with vec.Fori(NB // 2 - 1, NB - 1) as b:
                experts(b, LOOP, Weave(mixing(b + 1, NB)))
            experts(NB - 1, FINAL, Weave(iter(())))
            finish(NB - 1, 0)


_INS = ['x', 'c', 'positions', 'w_ada', 'b_ada', 'pre_mix_g', 'post_mix_g', 'w_in', 'conv_w', 'conv_b', 'dt_bias',
        'a_log', 'd_skip', 'ssd_norm_g', 'w_out', 'pre_ffn_g', 'post_ffn_g', 'peer_w_q', 'peer_sub_keys',
        'peer_u', 'peer_v']


def kernel(**inputs):
    import numpy as _np
    import concourse.bacc as _bacc
    from concourse import mybir as _mybir
    from concourse.bass_utils import run_bass_kernel_spmd as _run

    nc = _bacc.Bacc("TRN2", target_bir_lowering=False, num_devices=1)
    arrays, args = {}, []
    for name in _INS:
        a = _np.ascontiguousarray(inputs[name])
        arrays[f"in_{name}"] = a
        args.append(nc.dram_tensor(f"in_{name}", a.shape, _mybir.dt.from_np(a.dtype), kind="ExternalInput").ap())
    res = nc.dram_tensor("out_x", (1, SEQ, D), F32, kind="ExternalOutput").ap()
    hybrid_block(nc, *args, res)
    r = _run(nc, [arrays], core_ids=[0])
    return r.results[0]["out_x"]
```

```python
import math
from contextlib import ExitStack

import concourse.bass as bass
from concourse import mybir

ALU = mybir.AluOpType
ACT = mybir.ActivationFunctionType
AX = mybir.AxisListType
F32 = mybir.dt.float32
BF16 = mybir.dt.bfloat16
I32 = mybir.dt.int32
U32 = mybir.dt.uint32

P = 128
D = 1024
KC = D // P
SEQ = 1024
NB = SEQ // P
HD = 64
HEADS = 8
HALF = HD // 2
TOPK = 256
NSTATE = 128
CT = 8
TAPS = 4
EXPERT_KEYS = 128
PK = 16
LISTS = 2 * HEADS
SLOTS = HEADS * PK
THETA = 10000.0
EPS = 1e-6

C_QI = 768
C_KI = 1280
C_Z = 1352
C_XBC = 1864
C_DT = 2888
D_IN = 2896

NEG = -1e30
TAKEN = -3e38
LOW = -2e38

UR = 6
VR = 4
GR = 4
SHORT = TOPK // P
V_USED = SLOTS + 1
END = 1 << 30

G1, SC2, G2, SH2 = 2, 4, 5, 3
LATE_PARTS = (G1, SC2, G2, SH2)
LATE_IN = {1: 0, 2: 1, 3: 2, NB - 1: 3}

PHASES = ((-1, 6, 4, 0), (28, 7, 16, 0), (38, 9, 4, 0), (116, 8, 51, 0), (117, 8, 0, 0), (144, 40, 0, 8),
          (148, 11, 0, 2), (149, 4, 0, 1), (151, 2, 0, 1), (152, 2, 0, 1), (155, 2, 0, 1), (156, 2, 0, 1),
          (159.6, 8, 0, 2), (160, 1, 0, 1), (162, 4, 0, 1), (206, 14, 0, 29), (207, 0, 0, 5))
FIRST_PHASES = ((-1, 30, 0, 0), (28, 14, 0, 12), (116, 2, 0, 0), (144, 28, 0, 6),
                (148, 12, 0, 2), (149, 4, 0, 1), (156, 8, 0, 4), (159.6, 8, 0, 2), (160, 1, 0, 1), (162, 4, 0, 1),
                (206, 17, 0, 22), (207, 0, 0, 2))
LAST_PHASES = ((0, 17, 75, 0), (0, 8, 0, 0), (0, 103, 0, 93), (0, 0, 0, 35))
LEFT = sum(w for _, _, w, _ in PHASES)


def plan(phases):
    steps, done, stage = [], [0, 0, 0], -2.0
    for end, *counts in phases:
        base, total = list(done), sum(counts)
        for i in range(total):
            k = max(range(3), key=lambda k: (base[k] - done[k] + counts[k] * (i + 1) / total, -k))
            slot = done[k] + (SLOTS - LEFT if k == 1 else 0)
            done[k] += 1
            steps.append(("uwv"[k], slot, stage + (end - stage) * (i + 1) / total))
        stage = float(end)
    assert done[0] == SLOTS and done[1] in (0, LEFT) and done[2] in (SLOTS, SLOTS - LEFT)
    return steps


def moments(steps):
    at = {}
    u_steps = [i for i, step in enumerate(steps) if step[0] == "u"]
    for h in range(HEADS):
        n = h * PK + PK - 1 + UR
        i = u_steps[n] if n < SLOTS else min(u_steps[-1] + 4, len(steps) - 1)
        at.setdefault(i, []).append(("gelu", h))
        at.setdefault(i + 2, []).append(("weights", h))
    for i, (kind, slot, _) in enumerate(steps):
        if kind == "v" and slot % PK == 0:
            assert any(("weights", slot // PK) in at.get(j, ()) for j in range(i + 1)), slot
    first_v = next(i for i, step in enumerate(steps) if step[0] == "v")
    last_w = max([i for i, step in enumerate(steps) if step[0] == "w"] + [first_v - 9])
    at.setdefault(last_w + 1, []).append(("sum", 0))
    at.setdefault(last_w + 5, []).append(("finish", 0))
    at.setdefault(last_w + 14, []).append(("commit", 0))
    return at


class Signal:

    def __init__(self, sem, per=1, first=0):
        self.sem = sem
        self.per = per
        self.first = first

    def at(self, b, k):
        return b * self.per + (k - self.first * self.per)

    def wait(self, eng, b, k):
        value = self.at(b, k)
        if not (isinstance(value, int) and value == 0):
            eng.wait_ge(self.sem, value)


class Steps:

    def __init__(self, eng, sem):
        self.eng, self.sem, self.n = eng, sem, 0

    def begin(self):
        self.eng.sem_clear(self.sem)
        self.n = 0

    def __call__(self, ins):
        self.eng.wait_ge(self.sem, self.count(ins))

    def count(self, ins):
        self.n += 1
        ins.then_inc(self.sem, 1)
        return self.n

    def after(self, n):
        self.eng.wait_ge(self.sem, n)


class Weave:

    def __init__(self, gen):
        self.gen = gen
        self.stage = next(gen, END)

    def upto(self, stage):
        while self.stage <= stage:
            self.stage = next(self.gen, END)


def few_keys(b):
    return isinstance(b, int) and b < SHORT


def uses(ring, r):
    return len(range(r, SLOTS, ring))


def hybrid_block(nc, x, c, positions, w_ada, b_ada, pre_mix_g, post_mix_g, w_in, conv_w, conv_b, dt_bias,
                 a_log, d_skip, ssd_norm_g, w_out, pre_ffn_g, post_ffn_g, peer_w_q, peer_sub_keys,
                 peer_u, peer_v, out):
    ctx = ExitStack()
    with ctx:
        def sb(name, cols, dt=F32):
            return ctx.enter_context(nc.sbuf_tensor(name, [P, cols], dt))[:, :]

        def sem(name):
            return ctx.enter_context(nc.semaphore(name))

        def sig(name, per=1, first=0):
            return Signal(sem(name), per, first)

        def grid(ap, a):
            return ap.rearrange("p (a n) -> p a n", a=a)

        def over_last(ap, n):
            return ap.unsqueeze(2).to_broadcast([P, ap.shape[1], n])

        def over_first(ap, n):
            return ap.unsqueeze(1).to_broadcast([P, n, ap.shape[1]])

        ident = sb("ident", P)
        upto = sb("upto", P)
        after = sb("after", P)
        ones = sb("ones", P)
        causal = sb("causal", SEQ + 7 * P, BF16)
        iota_i = sb("iota_i", PK, I32)
        iota16 = sb("iota16", PK, BF16)
        inv_freq = sb("inv_freq", HALF)
        pos_i = sb("pos_i", NB, I32)
        pos_f = sb("pos_f", NB)
        eps = sb("eps", 1)
        convw = sb("convw", CT * TAPS)
        convb = sb("convb", CT)
        dtb = sb("dtb", HEADS)
        neg_a = sb("neg_a", HEADS)
        dskip = sb("dskip", HEADS)
        ssdg = sb("ssdg", 512)
        P1 = sb("P1", D)
        A2 = sb("A2", D)
        B2 = sb("B2", D)
        P2 = sb("P2", D)
        KV = sb("KV", 4 * SEQ)
        k0T, k1T, kiT = (KV[:, i * SEQ:(i + 1) * SEQ] for i in range(3))
        vv = grid(KV[:, 3 * SEQ:4 * SEQ], NB)
        keysT = grid(sb("keysT", HEADS * P), HEADS)
        W = sb("W", 16384 + 7168)
        w_in_sb = grid(W[:, 0:KC * D_IN], KC)
        w_out_sb = grid(W[:, 0:8192], KC)
        w_q_sb = grid(W[:, 8192:16384], KC)
        T = W[:, 16384:16384 + 7168]
        ring = sb("ring", (UR + VR) * D)
        u_ring = [ring[:, i * D:(i + 1) * D] for i in range(UR)]
        v_ring = [ring[:, (UR + i) * D:(UR + i + 1) * D] for i in range(VR)]
        diag = [sb(f"diag{i}", P) for i in range(GR)]
        HX = sb("HX", 4 * D)
        h2c, x1c, h2n, x1n = (HX[:, i * D:(i + 1) * D] for i in range(4))
        A1, B1 = h2c, x1c
        mix = sb("mix", D)
        state = sb("state", 512)
        hist = grid(sb("hist", CT * 3), CT)
        rowsum = sb("rowsum", 1)
        dtwi = sb("dtwi", NB * 16)
        dt_s = sb("dt_s", 64)
        adt = sb("adt", 64)
        eac = sb("eac", 64)
        dec = sb("dec", 64)
        etot = sb("etot", 64)
        wis = sb("wis", 64)
        scT = sb("scT", KC)
        stat = sb("stat", 16)
        negmax = sb("negmax", HEADS)
        psums = sb("psums", HEADS)
        rsums = sb("rsums", HEADS)
        mx8 = sb("mx8", 8)
        idxn = sb("idxn", SLOTS, U32)
        gn = sb("gn", SLOTS)
        idxu = sb("idxu", SLOTS, U32)
        idxv = sb("idxv", SLOTS, U32)
        gc = sb("gc", SLOTS)
        gsum = sb("gsum", HEADS)
        dots = sb("dots", SLOTS)
        gel = sb("gel", SLOTS)
        wgt = sb("wgt", SLOTS)

        ada_buf = [ring[:, i * 2048:(i + 1) * 2048] for i in range(4)]
        b_row = KV[0:1, 0:2 * D]
        late_buf = [ring[:, 6400 + i * D:6400 + (i + 1) * D] for i in range(2)]
        late_acc = B2
        keys_raw = grid(KV[:, 3072:4096], HEADS)
        cosT = ring[:, 9216:9472]
        sinT = ring[:, 9472:9728]
        ang = ring[:, 9728:9984]
        ang2 = ring[:, 9984:10240]
        hT = grid(ring[:, 0:D], KC)
        stag = ring[:, D:D + 2560]
        raw = ring[:, 3584:4992]
        rot = ring[:, 4992:6400]
        rtmp = mix[:, 0:704]
        small = T[:, 4480:4480 + 6 * 64]
        qT = grid(T[:, 0:512], 4)
        qiT = grid(T[:, 512:1024], 4)
        xc = grid(T[:, 1024:1024 + CT * 131], CT)
        L = T[:, 1024:2048]
        cv = grid(T[:, 2072:3096], CT)
        ctmp = grid(T[:, 3096:4120], CT)
        xtok = T[:, 3096:3608]
        btok = T[:, 3608:3864]
        xdt = T[:, 3864:4376]
        xw = T[:, 4376:4888]
        gh = grid(T[:, 4888:5400], 4)
        yy = T[:, 5400:5912]
        ytmp = T[:, 5912:6424]
        cbm = grid(T[:, 6424:6680], 2)
        zt = mix[:, 512:1024]
        SC = T[:, 1024:2048]
        AM = T[:, 2048:3072]
        RL = [T[:, 3072:4096], T[:, 4096:5120]]
        PT = grid(T[:, 5120:6144], NB)
        mixT = grid(T[:, 0:1024], KC)
        otmp = T[:, 1024:2048]
        h2T = grid(T[:, 2048:3072], KC)
        qpT = grid(T[:, 3072:4096], HEADS)
        ss = T[:, 4096:6144]
        cand = T[:, 0:2048]
        hot = T[:, 2048:3072].bitcast(BF16)
        sv = T[:, 6144:6400]
        si = T[:, 6400:6656].bitcast(U32)
        sif = T[:, 6656:6784].bitcast(BF16)
        fv = T[:, 6912:7040]
        fp = T[:, 7040:7168].bitcast(U32)
        fpi = T[:, 4096:4224].bitcast(U32)
        fpf = T[:, 4224:4288].bitcast(BF16)
        e2 = T[:, 3072:3200]
        e1 = T[:, 4352:4480]

        ps = ctx.enter_context(nc.psum_tensor("ps", [P, 8 * 512], F32))[:, :]

        def bank(i, n=1):
            return ps[:, i * 512:(i + n) * 512]

        VB, SB, TB, OB, XB = bank(0, 2), bank(2, 2), bank(4, 2), bank(6), bank(7)

        spill = nc.dram_tensor("spill", [NB, P, 2560], F32, kind="Internal").ap()

        s_consts = sem("consts_ready")
        s_conststep = sem("const_steps")
        s_small = sem("small_in")
        s_rows = sem("c_positions_in")
        s_gain0 = sem("pre_mix_gain_in")
        s_gain = sem("gain_in")
        s_brow = sem("b_ada_in")
        s_laterow = sem("b_ada_late_in")
        s_keys = sem("keys_in")
        s_ada = [sem(f"ada_in{i}") for i in range(4)]
        s_wide = sem("silu_c_wide")
        s_silu = sem("silu_c")
        s_adaused = sem("ada_used")
        s_lateclear = sem("ada_late_clear")
        s_lateused = sem("ada_late_used")
        s_latepsum = sem("ada_late_psum")
        s_mod = sem("mod_done")
        s_keyps = sem("keys_psum")
        s_keysT = sem("keys_T")
        s_ang = sem("angles_ready")
        s_trig = sem("trig_ready")
        s_win = [sem(f"w_in_in{i}") for i in range(4)]
        s_wout = sem("w_out_in")
        s_wq = sem("w_q_in")

        a_x = sig("a_x_in", 16)
        a_sumsq = sig("a_x_sumsq")
        a_root = sig("a_x_root")
        a_h = sig("a_h")
        a_hps = sig("a_hT_psum")
        a_hT = sig("a_hT")
        a_proj = sig("a_proj", 6)
        a_raw = sig("a_raw")
        a_z = sig("a_z")
        a_rope = sig("a_rope")
        a_rps = sig("a_rot_psum")
        a_rot = sig("a_rot")
        a_xbc = sig("a_xbc")
        a_out = sig("a_spilled", 16)
        s_dtv = sem("dt_vector")
        s_dta = sem("dt_scalar")
        s_dtp = sem("dt_psum")

        m_xbc = sig("m_xbc_in", 16)
        m_z = sig("m_z_in", 16)
        m_qq = sig("m_qq_in", 16)
        m_x = sig("m_x_in", 16)
        conv = sig("conv_done")
        convact = sig("conv_silu", CT)
        zgate = sig("z_silu")
        chanT = sig("channels_psum", 2)
        tok = sig("tokens_ready")
        xwr = sig("xw_ready")
        ghr = sig("gh_ready", 2)
        cbps = sig("cb_psum")
        seg = sig("seg_psum", 2)
        decay = sig("decay_ready", 2)
        masked = sig("masked_ready", 2)
        yoff = sig("yoff_psum")
        stps = sig("state_psum")
        ydiag = sig("ydiag_psum")
        stdone = sig("state_done")
        gated = sig("gated")
        ssdrms = sig("ssd_root")
        ssdout = sig("ssd_out")
        logit = sig("index_psum", HEADS, SHORT)
        relu = sig("index_relu", HEADS, SHORT)
        scacc = sig("index_summed", HEADS, SHORT)
        sps = sig("scores_psum", HEADS)
        sread = sig("scores_read", HEADS)
        smax = sig("max_ready", HEADS)
        sexp = sig("probs_ready", HEADS)
        ptps = sig("probsT_psum", HEADS)
        ptc = sig("probsT_ready", HEADS)
        av = sig("av_psum", HEADS)
        mixr = sig("mix_ready")
        mixps = sig("mixT_psum")
        mixTr = sig("mixT_ready")
        outps = sig("out_psum")
        outrms = sig("out_root")
        x1r = sig("x1_ready")
        x1rms = sig("x1_root")
        h2r = sig("h2_ready")
        h2ps = sig("h2T_psum")
        h2Tr = sig("h2T_ready")
        pqps = sig("peer_q_psum")
        pqr = sig("peer_q_ready")
        pss = sig("sub_scores_psum")
        s2 = sig("sub_scores_ready", 2)
        fvr = sig("top_scores_ready")
        gexp = sig("gate_exp")
        prep = sig("experts_chosen")
        idxc = sig("indices_taken", 2)
        dot = sig("dot_done", SLOTS)
        gelu = sig("gelu_done", HEADS)
        wready = sig("weights_ready", HEADS)
        dg = sig("diag_ready", SLOTS)
        vused = sig("v_used", V_USED)
        frsum = sig("f_sumsq")
        frms = sig("f_root")
        xfin = sig("x_final")
        xcommit = sig("x1_taken")
        xout = sig("x_out", 16)
        u_in = [sem(f"u_in{r}") for r in range(UR)]
        v_in = [sem(f"v_in{r}") for r in range(VR)]
        vstep = sem("vector_steps")
        pstep = sem("vector_expert_steps")
        astep = sem("scalar_steps")
        bstep = sem("vector_setup_steps")
        rstep = sem("vector_projection_steps")

        s_room = sem("room_seen")
        s_turn = sem("turn_seen")

        FIRST, LOOP, FINAL = plan(FIRST_PHASES), plan(PHASES), plan(LAST_PHASES)

        block = ctx.enter_context(nc.Block())

        @block.sync
        def _(sp):
            x_blocks = x.rearrange("o (b p) d -> b p (o d)", p=P)
            out_blocks = out.rearrange("o (b p) d -> b p (o d)", p=P)
            sp.dma_start(scT, c.rearrange("o (k p) -> p (o k)", p=P), allow_slow_non_contiguous=True).then_inc(s_rows, 16)
            sp.dma_start(pos_i, positions.rearrange("o (b p) -> p (o b)", p=P), allow_slow_non_contiguous=True).then_inc(s_rows, 16)
            sp.dma_start(b_row, b_ada[0:1, 0:2 * D]).then_inc(s_brow, 16)
            w_in_cols = w_in[0].rearrange("(k p) n -> p k n", p=P)

            def load_w_in(i, *spans):
                for lo, hi in spans:
                    sp.dma_start(w_in_sb[:, :, lo:hi], w_in_cols[:, :, lo:hi]).then_inc(s_win[i], 16)

            for k in range(KC):
                if k >= 4:
                    sp.wait_ge(s_adaused, k - 3)
                sp.dma_start(ada_buf[k % 4], w_ada[0, k * P:(k + 1) * P, 0:2 * D]).then_inc(s_ada[k % 4], 16)
                if k == 3:
                    sp.dma_start(A1, pre_mix_g[0, :].partition_broadcast(P)).then_inc(s_gain0, 16)
            load_w_in(0, (C_Z, C_XBC))
            load_w_in(1, (0, 512))
            load_w_in(2, (512, 1024))
            load_w_in(3, (1024, C_Z), (C_XBC, D_IN))
            for dst, src in ((P1, post_mix_g), (A2, pre_ffn_g), (P2, post_ffn_g), (ssdg, ssd_norm_g)):
                sp.dma_start(dst, src[0, :].partition_broadcast(P)).then_inc(s_gain, 16)

            def store_staging(b):
                a_rot.wait(sp, b, 1)
                a_xbc.wait(sp, b, 1)
                sp.dma_start(spill[b], stag).then_inc(a_out.sem, 16)

            def late_loads(part, lo, hi):
                cols = slice(LATE_PARTS[part] * D, (LATE_PARTS[part] + 1) * D)
                if lo == 0:
                    sp.wait_ge(s_lateclear, part + 1)
                    sp.dma_start(late_acc[0:1, :], b_ada[0:1, cols]).then_inc(s_laterow, 16)
                for k in range(lo, hi):
                    n = part * KC + k
                    if n >= 2:
                        sp.wait_ge(s_lateused, n - 1)
                    sp.dma_start(late_buf[n % 2], w_ada[0, k * P:(k + 1) * P, cols]).then_inc(s_ada[n % 2], 16)

            sp.wait_ge(s_adaused, KC)
            for b in range(4):
                if b:
                    late_loads(b - 1, 2, KC)
                if b < 3:
                    late_loads(b, 0, 2)
                store_staging(b)
            late_loads(3, 0, 2)
            with sp.Fori(4, NB - 1) as b:
                store_staging(b)
            late_loads(3, 2, KC)
            a_out.wait(sp, 1, 0)
            a_proj.wait(sp, NB, 0)

            def xbc_load(b):
                prep.wait(sp, b, 0)
                sp.dma_start(xc[:, :, 3:131], spill[b, :, 1536:2560].rearrange("p (a n) -> p a n", a=CT))\
                    .then_inc(m_xbc.sem, 16)

            def qz_loads(b):
                sp.dma_start(zt, spill[b, :, 1024:1536]).then_inc(m_z.sem, 16)
                sp.dma_start(T[:, 0:1024], spill[b, :, 0:1024]).then_inc(m_qq.sem, 16)

            def x_load(b):
                xcommit.wait(sp, b, 0)
                sp.dma_start(x1n, x_blocks[b]).then_inc(m_x.sem, 16)

            def peer_store(b):
                xfin.wait(sp, b, 1)
                sp.dma_start(out_blocks[b], x1c).then_inc(xout.sem, 16)

            xbc_load(0)
            a_rot.wait(sp, NB, 0)
            store_staging(NB - 1)
            qz_loads(0)
            a_out.wait(sp, NB, 0)
            x_load(0)
            sp.dma_start(w_out_sb, w_out[0].rearrange("(k p) n -> p k n", p=P)).then_inc(s_wout, 16)
            sp.dma_start(w_q_sb, peer_w_q[0].rearrange("(k p) n -> p k n", p=P)).then_inc(s_wq, 16)
            xbc_load(1)
            qz_loads(1)
            x_load(1)
            with sp.Fori(1, NB - 1) as b:
                xbc_load(b + 1)
                qz_loads(b + 1)
                xfin.wait(sp, b, 0)
                sp.dma_start(out_blocks[b - 1], x1c).then_inc(xout.sem, 16)
                x_load(b + 1)
            peer_store(NB - 2)
            peer_store(NB - 1)
            xout.wait(sp, NB, 0)

        @block.gpsimd
        def _(pool):
            n = 0

            def made(ins):
                nonlocal n
                n += 1
                ins.then_inc(s_conststep, 1)
                pool.wait_ge(s_conststep, n)

            x_blocks = x.rearrange("o (b p) d -> b p (o d)", p=P)
            pool.dma_start(x1n, x_blocks[0]).then_inc(a_x.sem, 16)
            made(pool.memset(eps, EPS))
            made(pool.memset(ident, 0.0))
            made(pool.affine_select(out=ident, in_=ident, compare_op=ALU.not_equal, fill=1.0, base=0,
                                    pattern=[[-1, P]], channel_multiplier=1))
            made(pool.memset(ones, 1.0))
            made(pool.affine_select(out=upto, in_=ones, compare_op=ALU.is_ge, fill=0.0, base=0,
                                    pattern=[[1, P]], channel_multiplier=-1))
            made(pool.affine_select(out=after, in_=ones, compare_op=ALU.is_gt, fill=0.0, base=0,
                                    pattern=[[-1, P]], channel_multiplier=1))
            pool.sem_inc(s_consts, 1)
            made(pool.iota(iota_i, pattern=[[1, PK]], base=0, channel_multiplier=0))
            for i in range(HALF):
                made(pool.memset(inv_freq[:, i:i + 1], float(THETA ** (-2.0 * i / HD))))
            made(pool.memset(state, 0.0))
            made(pool.memset(hist.rearrange("p a n -> p (a n)"), 0.0))
            made(pool.memset(causal, 0.0))
            made(pool.affine_select(out=causal, in_=causal, compare_op=ALU.is_ge, fill=NEG, base=7 * P,
                                    pattern=[[-1, SEQ + 7 * P]], channel_multiplier=1))
            pool.sem_inc(s_consts, 1)
            pool.dma_start(convb, conv_b[0].rearrange("(c p) -> p c", p=P), allow_slow_non_contiguous=True).then_inc(s_small, 16)
            pool.dma_start(convw, conv_w[0].rearrange("j (c p) -> p (j c)", p=P),
                           allow_slow_non_contiguous=True).then_inc(s_small, 16)
            pool.dma_start(dtb, dt_bias[0, :].partition_broadcast(P)).then_inc(s_small, 16)
            pool.dma_start(neg_a, a_log[0, :].partition_broadcast(P)).then_inc(s_small, 16)
            pool.dma_start(dskip, d_skip[0, :].partition_broadcast(P)).then_inc(s_small, 16)
            pool.dma_start(keys_raw.rearrange("p h (t d) -> p h t d", t=2),
                           peer_sub_keys[0].rearrange("h t k d -> k h t d")).then_inc(s_keys, 16)
            with pool.Fori(1, NB) as b:
                a_h.wait(pool, b, 0)
                pool.dma_start(x1n, x_blocks[b]).then_inc(a_x.sem, 16)

            def experts(b, steps):
                prep.wait(pool, b, 1)
                dot.wait(pool, b, 0)
                pool.sem_inc(s_room, 1)
                pool.tensor_copy(idxu, idxn).then_inc(idxc.sem, 1)
                idxc.wait(pool, b, 1)
                pool.sem_inc(s_room, 1)
                for kind, n, _ in steps:
                    if kind == "u":
                        r = n % UR
                        if n >= UR:
                            dot.wait(pool, b, n - UR + 1)
                            pool.sem_inc(s_room, 1)
                        pool.indirect_dma_start(
                            out=u_ring[r], out_offset=None, in_=peer_u[0],
                            in_offset=bass.IndirectOffsetOnAxis(ap=idxu[:, n:n + 1], axis=0),
                        ).then_inc(u_in[r], 16)
                    else:
                        back = SLOTS if kind == "w" else 0
                        if n == 0:
                            vused.wait(pool, b, 0)
                            pool.sem_inc(s_room, 1)
                            pool.tensor_copy(idxv, idxn).then_inc(idxc.sem, 1)
                            idxc.wait(pool, b, 2)
                            pool.sem_inc(s_room, 1)
                        r = n % VR
                        if n >= VR:
                            vused.wait(pool, b, n - VR + 1 - (V_USED if back else 0))
                            pool.sem_inc(s_room, 1)
                        pool.indirect_dma_start(
                            out=v_ring[r], out_offset=None, in_=peer_v[0],
                            in_offset=bass.IndirectOffsetOnAxis(ap=idxv[:, n:n + 1], axis=0),
                        ).then_inc(v_in[r], 16)

            experts(0, FIRST)
            with pool.Fori(1, NB - 1) as b:
                experts(b, LOOP)
            experts(NB - 1, FINAL)

        @block.scalar
        def _(act):
            steps = Steps(act, astep)
            sc = nc.scalar
            act.wait_ge(s_rows, 32)
            sc.activation(scT, scT, ACT.Silu).then_inc(s_silu, 1)
            act.wait_ge(s_consts, 1)

            def x_stat(b, k):
                a_x.wait(act, b, 16 * k)
                a_hps.wait(act, b, k - 1)
                sc.activation(h2n, x1n, ACT.Square, accum_out=rowsum).then_inc(a_sumsq.sem, 1)
                a_sumsq.wait(act, b, k)
                sc.activation(rowsum, rowsum, ACT.Sqrt, scale=1.0 / D, bias=eps).then_inc(a_root.sem, 1)

            x_stat(0, 1)
            act.wait_ge(s_small, 16 * 5)
            act.wait_ge(s_ang, 1)
            sc.activation(sinT, sinT, ACT.Sin)
            sc.activation(cosT, cosT, ACT.Sin).then_inc(s_trig, 1)

            def copy_h(b, k):
                a_hps.wait(act, b, k)
                sc.copy(hT.rearrange("p a n -> p (a n)"), bank(0, 2)).then_inc(a_hT.sem, 1)

            def project(b, more):
                if more:
                    x_stat(b, 2)
                a_rope.wait(act, b, 0)
                a_proj.wait(act, b, 2)
                sc.copy(raw[:, 0:512], bank(2))
                a_proj.wait(act, b, 3)
                kk = bank(3)[:, 0:128].rearrange("p (g d) -> p g d", g=2)
                for twice in range(2):
                    sc.copy(raw[:, 512:768].rearrange("p (g t d) -> p g t d", g=2, t=2)[:, :, twice, :], kk)
                if not few_keys(b):
                    sc.copy(raw[:, 896:1152], bank(3)[:, 256:512])
                sc.copy(vv[:, b, :], bank(3)[:, 128:256])
                a_proj.wait(act, b, 4)
                if not few_keys(b):
                    sc.copy(raw[:, 1152:1408], bank(4)[:, 0:256])
                for twice in range(2):
                    sc.copy(raw[:, 768 + 64 * twice:832 + 64 * twice], bank(4)[:, 256:320])
                sc.copy(grid(dtwi, NB)[:, b, :], bank(4)[:, 320:336]).then_inc(a_raw.sem, 1)
                a_out.wait(act, b, 0)
                sc.copy(stag[:, 1024:1536], bank(5)).then_inc(a_z.sem, 1)
                if more:
                    copy_h(b, 2)
                a_rps.wait(act, b, 1)
                sc.copy(stag[:, 0:512], bank(2))
                if not few_keys(b):
                    sc.copy(stag[:, 512:1024], bank(3))
                for i, kT in enumerate((k0T, k1T, kiT)):
                    last = sc.copy(grid(kT, NB)[:, b, :], bank(4)[:, i * P:(i + 1) * P])
                last.then_inc(a_rot.sem, 1)

            copy_h(0, 1)
            for b in range(4):
                project(b, True)
            with act.Fori(4, NB - 1) as b:
                project(b, True)
            project(NB - 1, False)

            act.wait_ge(s_dtv, 1)
            sc.activation(small[:, 0:64], small[:, 0:64], ACT.Exp, scale=-1.0)
            sc.activation(neg_a, neg_a, ACT.Exp).then_inc(s_dta, 1)
            act.wait_ge(s_dtv, 2)
            sc.activation(small[:, 64:128], small[:, 64:128], ACT.Ln).then_inc(s_dta, 1)
            act.wait_ge(s_dtv, 4)
            sc.activation(eac, XB[:, 0:64], ACT.Exp)
            sc.activation(etot, XB[:, 64:128], ACT.Exp)
            sc.activation(dec, small[:, 0:64], ACT.Exp).then_inc(s_dta, 1)

            def root(col, width):
                return sc.activation(stat[:, col:col + 1], stat[:, col:col + 1], ACT.Sqrt,
                                     scale=1.0 / width, bias=eps)

            def mixing(b, nb):
                steps.begin()
                yield 8
                conv.wait(act, b, 1)
                for t in range(CT):
                    sc.activation(cv[:, t, :], cv[:, t, :], ACT.Silu, bias=convb[:, t:t + 1])\
                        .then_inc(convact.sem, 1)
                yield 10
                m_z.wait(act, b, 16)
                sc.activation(zt, zt, ACT.Silu).then_inc(zgate.sem, 1)
                for g in range(2):
                    yield 17 + 2 * g
                    seg.wait(act, b, g + 1)
                    sc.activation(L[:, g * 512:(g + 1) * 512], bank(2 + g), ACT.Exp).then_inc(decay.sem, 1)
                yield 27
                gated.wait(act, b, 1)
                steps(sc.activation(ytmp, yy, ACT.Square, accum_out=stat[:, 0:1]))
                root(0, 512).then_inc(ssdrms.sem, 1)
                nk = nb * P
                yield 28
                ssdout.wait(act, b, 1)
                for h in range(HEADS if nb > SHORT else 0):
                    yield 29 + h
                    if h >= 2:
                        scacc.wait(act, b, h - 1)
                    logit.wait(act, b, h + 1)
                    sc.activation(RL[h % 2][:, 0:nk], (SB if h % 2 == 0 else TB)[:, 0:nk], ACT.Relu, scale=HD ** -0.5)\
                        .then_inc(relu.sem, 1)
                for h in range(HEADS + 1):
                    if h < HEADS:
                        yield 118 + 3 * h
                        smax.wait(act, b, h + 1)
                        sc.activation(RL[h % 2][:, 0:nk], RL[h % 2][:, 0:nk], ACT.Exp, bias=negmax[:, h:h + 1],
                                      accum_out=psums[:, h:h + 1]).then_inc(sexp.sem, 1)
                    yield 119 + 3 * h
                    if h < HEADS:
                        ptps.wait(act, b, h + 1)
                        if h:
                            av.wait(act, b, h)
                        sc.copy(PT.rearrange("p a n -> p (a n)")[:, 0:nk], TB[:, 0:nk]).then_inc(ptc.sem, 1)
                yield 145
                mixps.wait(act, b, 1)
                sc.copy(mixT.rearrange("p a n -> p (a n)"), TB).then_inc(mixTr.sem, 1)
                yield 148
                outps.wait(act, b, 1)
                steps(sc.activation(otmp, SB, ACT.Square, accum_out=stat[:, 1:2]))
                root(1, D).then_inc(outrms.sem, 1)
                yield 151
                x1r.wait(act, b, 1)
                steps(sc.activation(otmp, x1n, ACT.Square, accum_out=stat[:, 2:3]))
                root(2, D).then_inc(x1rms.sem, 1)
                yield 156
                h2ps.wait(act, b, 1)
                sc.copy(h2T.rearrange("p a n -> p (a n)"), TB).then_inc(h2Tr.sem, 1)
                yield 160
                pqps.wait(act, b, 1)
                sc.copy(qpT.rearrange("p a n -> p (a n)"), SB).then_inc(pqr.sem, 1)
                yield 161
                pss.wait(act, b, 1)
                sc.copy(ss[:, 0:1024], SB).then_inc(s2.sem, 1)
                sc.copy(ss[:, 1024:2048], TB).then_inc(s2.sem, 1)
                yield 196
                fvr.wait(act, b, 1)
                sc.activation(gn, gn, ACT.Exp).then_inc(gexp.sem, 1)

            def finish(b, back):
                vused.wait(act, b, V_USED - back * V_USED)
                sc.activation(PT.rearrange("p a n -> p (a n)"), VB, ACT.Square, accum_out=stat[:, 3:4])\
                    .then_inc(frsum.sem, 1)
                frsum.wait(act, b, 1 - back)
                root(3, D).then_inc(frms.sem, 1)

            def experts(b, plan_steps, weave):
                at = moments(plan_steps)
                for i in range(len(plan_steps)):
                    kind, n, stage = plan_steps[i]
                    for what, h in at.get(i, ()):
                        if what == "gelu":
                            s = slice(h * PK, (h + 1) * PK)
                            dot.wait(act, b, (h + 1) * PK)
                            sc.activation(gel[:, s], dots[:, s], ACT.Gelu).then_inc(gelu.sem, 1)
                        if what == "sum" and plan_steps is not FIRST:
                            finish(b, 1)
                    if kind != "u":
                        back = SLOTS if kind == "w" else 0
                        if kind == "v":
                            wready.wait(act, b, n // PK + 1)
                        if n >= GR or kind == "w":
                            vused.wait(act, b, n - GR + 1 - (V_USED if back else 0))
                        sc.activation(diag[n % GR], ident, ACT.Copy, scale=wgt[:, n:n + 1]).then_inc(dg.sem, 1)
                    weave.upto(stage)
                weave.upto(END - 1)
                wready.wait(act, b, HEADS)

            Weave(mixing(0, 1)).upto(END - 1)
            experts(0, FIRST, Weave(mixing(1, 2)))
            with act.Fori(1, NB // 2 - 1) as b:
                experts(b, LOOP, Weave(mixing(b + 1, NB // 2)))
            with act.Fori(NB // 2 - 1, NB - 1) as b:
                experts(b, LOOP, Weave(mixing(b + 1, NB)))
            experts(NB - 1, FINAL, Weave(iter(())))
            finish(NB - 1, 0)

        @block.tensor
        def _(pe):
            te = nc.tensor

            def turn(dst, src, tiles):
                for i in range(tiles):
                    last = te.transpose(dst[:, i * P:(i + 1) * P], src[:, i * P:(i + 1) * P], ident)
                return last

            def turn_rows(dst, src, tiles):
                for i in range(tiles):
                    last = te.transpose(dst[:, i * P:(i + 1) * P], src[:, i, :], ident)
                return last

            pe.wait_ge(s_consts, 1)
            pe.wait_ge(s_wide, 1)
            wide = grid(mix, KC)
            pe.wait_ge(s_brow, 16)
            for j in range(4):
                te.matmul(bank(j), ones[0:1, :], b_row[:, j * 512:(j + 1) * 512], start=True, stop=False)
            for k in range(KC):
                pe.wait_ge(s_ada[k % 4], 16 * (k // 4 + 1))
                for j in range(4):
                    last = te.matmul(bank(j), wide[:, k, :], ada_buf[k % 4][:, j * 512:(j + 1) * 512],
                                     start=False, stop=(k == KC - 1))
                last.then_inc(s_adaused, 1)
            pe.wait_ge(s_keys, 16)
            turn_rows(bank(4, 2), keys_raw, HEADS).then_inc(s_keyps, 1)
            pe.wait_ge(s_mod, 1)
            pe.wait_ge(s_keysT, 1)

            def sum_late(part):
                pe.wait_ge(s_mod, 1 + part)
                pe.wait_ge(s_lateused, KC * (part + 1))
                for j in range(2):
                    last = te.matmul(bank(j), ones, late_acc[:, j * 512:(j + 1) * 512], start=True, stop=True)
                last.then_inc(s_latepsum, 1)

            def turn_h(b, k):
                a_h.wait(pe, b, k)
                turn(bank(0, 2), h2n, KC).then_inc(a_hps.sem, 1)

            def project(b, more):
                a_hT.wait(pe, b, 1)
                a_z.wait(pe, b, 0)
                groups = [((5, 0, 512, C_Z),), ((2, 0, 512, 0),), ((3, 0, 512, 512),),
                          ((4, 0, C_Z - 1024, 1024), (4, C_Z - 1024, 8, C_DT))]
                if few_keys(b):
                    groups[2] = ((3, 0, C_QI - 512, 512),)
                    groups[3] = ((4, C_KI - 1024, C_Z - C_KI, C_KI), (4, C_Z - 1024, 8, C_DT))
                late = LATE_IN.get(b) if isinstance(b, int) else None
                for n, parts in enumerate(groups):
                    if isinstance(b, int) and b == 0:
                        pe.wait_ge(s_win[n], 32 if n == 3 else 16)
                    if n == 1:
                        a_rot.wait(pe, b, 0)
                    for i, at, width, col in parts:
                        for k in range(KC):
                            last = te.matmul(bank(i)[:, at:at + width], hT[:, k, :], w_in_sb[:, k, col:col + width],
                                             start=(k == 0), stop=(k == KC - 1))
                    last.then_inc(a_proj.sem, 1)
                    if late is not None and n == 3:
                        sum_late(late)
                a_xbc.wait(pe, b, 0)
                for t in range(CT):
                    for k in range(KC):
                        last = te.matmul(bank(6 + t // 4)[:, t % 4 * P:(t % 4 + 1) * P],
                                         w_in_sb[:, k, C_XBC + t * P:C_XBC + (t + 1) * P], hT[:, k, :],
                                         start=(k == 0), stop=(k == KC - 1))
                    if t % 4 == 3:
                        last.then_inc(a_proj.sem, 1)
                if more:
                    if late is not None:
                        pe.wait_ge(s_mod, 2 + late)
                    turn_h(b, 2)
                a_rope.wait(pe, b, 1)
                a_raw.wait(pe, b, 1)
                turn(bank(2), rot, 4)
                if not few_keys(b):
                    turn(bank(3), rot[:, 896:1408], 4)
                turn(bank(4), rot[:, 512:896], 3).then_inc(a_rps.sem, 1)

            turn_h(0, 1)
            for b in range(4):
                project(b, True)
            with pe.Fori(4, NB - 1) as b:
                project(b, True)
            project(NB - 1, False)

            a_rot.wait(pe, NB, 0)
            pe.wait_ge(s_dtv, 3)
            a_xbc.wait(pe, NB, 0)
            te.matmul(XB[:, 0:64], upto, adt, start=True, stop=True)
            te.matmul(XB[:, 64:128], ones, adt, start=True, stop=True).then_inc(s_dtp, 1)

            def mixing(b, nb):
                yield 12
                convact.wait(pe, b, CT)
                for t in range(4):
                    last = te.transpose(XB[:, t * P:(t + 1) * P], cv[:, t, :], ident)
                last.then_inc(chanT.sem, 1)
                for t in range(2):
                    last = te.transpose(OB[:, t * P:(t + 1) * P], cv[:, 4 + t, :], ident)
                last.then_inc(chanT.sem, 1)
                for g in range(2):
                    last = te.matmul(bank(4)[:, g * P:(g + 1) * P], cv[:, 4 + g, :], cv[:, 6 + g, :],
                                     start=True, stop=True)
                last.then_inc(cbps.sem, 1)
                for g in range(2):
                    yield 16 + 2 * g
                    ghr.wait(pe, b, g + 1)
                    for i in range(4):
                        last = te.matmul(bank(2 + g)[:, i * P:(i + 1) * P], gh[:, i, :], upto, start=True, stop=True)
                    last.then_inc(seg.sem, 1)
                yield 18
                tok.wait(pe, b, 1)
                stdone.wait(pe, b, 0)
                for g in range(2):
                    last = te.matmul(OB[:, g * 256:(g + 1) * 256], cv[:, 6 + g, :], state[:, g * 256:(g + 1) * 256],
                                     start=True, stop=True)
                last.then_inc(yoff.sem, 1)
                xwr.wait(pe, b, 1)
                for g in range(2):
                    last = te.matmul(XB[:, g * 256:(g + 1) * 256], btok[:, g * P:(g + 1) * P],
                                     xw[:, g * 256:(g + 1) * 256], start=True, stop=True)
                last.then_inc(stps.sem, 1)
                for g in range(2):
                    yield 21 + 2 * g
                    masked.wait(pe, b, g + 1)
                    for h in range(4 * g, 4 * g + 4):
                        last = te.matmul(bank(5)[:, h * HD:(h + 1) * HD], L[:, h * P:(h + 1) * P],
                                         xdt[:, h * HD:(h + 1) * HD], start=True, stop=True)
                last.then_inc(ydiag.sem, 1)
                m_qq.wait(pe, b, 16)
                nk = nb * P
                wide_steps = [slice(at, min(at + 512, nk)) for at in range(0, nk, 512)]
                yield 28
                gated.wait(pe, b, 1)
                for h in range(HEADS if nb > SHORT else 0):
                    yield 28 + h
                    if h >= 2:
                        relu.wait(pe, b, h - 1)
                    dst = SB if h % 2 == 0 else TB
                    half = slice(h % 2 * HD, h % 2 * HD + HD)
                    for part in wide_steps:
                        last = te.matmul(dst[:, part], qiT[half, h // 2, :], kiT[half, part], start=True, stop=True)
                    last.then_inc(logit.sem, 1)

                def scores(h):
                    if h:
                        sread.wait(pe, b, h)
                    elif nb > SHORT:
                        relu.wait(pe, b, HEADS)
                    half = slice(h % 2 * HD, h % 2 * HD + HD)
                    kT = (k0T, k1T)[h // 4]
                    for part in wide_steps:
                        last = te.matmul(SB[:, part], qT[half, h // 2, :], kT[half, part], start=True, stop=True)
                    last.then_inc(sps.sem, 1)

                def values(h):
                    ptc.wait(pe, b, h + 1)
                    for j in range(nb):
                        last = te.matmul(OB[:, h * HD:(h + 1) * HD], PT[:, j, :],
                                         vv[:, j, h // 4 * HD:(h // 4 + 1) * HD], start=(j == 0), stop=(j == nb - 1))
                    last.then_inc(av.sem, 1)

                yield 110
                scores(0)
                for h in range(HEADS):
                    yield 118 + 3 * h
                    if h < HEADS - 1:
                        scores(h + 1)
                    sexp.wait(pe, b, h + 1)
                    if h:
                        ptc.wait(pe, b, h)
                    turn(TB, RL[h % 2], nb).then_inc(ptps.sem, 1)
                    if h:
                        yield 119 + 3 * h
                        values(h - 1)
                yield 142
                values(HEADS - 1)
                yield 144
                mixr.wait(pe, b, 1)
                turn(TB, mix, KC).then_inc(mixps.sem, 1)
                for j in range(2):
                    if j == 0:
                        yield 145
                        mixTr.wait(pe, b, 1)
                        pe.wait_ge(s_wout, 16)
                    for k in range(KC):
                        yield 145 + (j * KC + k) / 5
                        last = te.matmul(SB[:, j * 512:(j + 1) * 512], mixT[:, k, :],
                                         w_out_sb[:, k, j * 512:(j + 1) * 512], start=(k == 0), stop=(k == KC - 1))
                last.then_inc(outps.sem, 1)
                yield 155
                h2r.wait(pe, b, 1)
                turn(TB, h2n, KC).then_inc(h2ps.sem, 1)
                yield 156
                h2Tr.wait(pe, b, 1)
                pe.wait_ge(s_wq, 16)
                for h in range(HEADS):
                    yield 156 + h / 2
                    for k in range(KC):
                        last = te.matmul(SB[:, h * P:(h + 1) * P], w_q_sb[:, k, h * P:(h + 1) * P], h2T[:, k, :],
                                         start=(k == 0), stop=(k == KC - 1))
                last.then_inc(pqps.sem, 1)
                yield 160
                pqr.wait(pe, b, 1)
                for i in range(LISTS):
                    half = slice(i // HEADS * HD, i // HEADS * HD + HD)
                    last = te.matmul(bank(2 + i // 4)[:, i % 4 * P:(i % 4 + 1) * P], qpT[half, i % HEADS, :],
                                     keysT[half, i % HEADS, :], start=True, stop=True)
                last.then_inc(pss.sem, 1)

            def experts(b, plan_steps, weave):
                for kind, n, stage in plan_steps:
                    if kind != "u":
                        back = SLOTS if kind == "w" else 0
                        r = n % VR
                        if n == 0:
                            xfin.wait(pe, b, 0)
                        dg.wait(pe, b, n + 1 - back)
                        pe.wait_ge(v_in[r], 16 * (b * uses(VR, r) + n // VR + 1 - back // VR))
                        for j in range(2):
                            last = te.matmul(VB[:, j * 512:(j + 1) * 512], diag[n % GR],
                                             v_ring[r][:, j * 512:(j + 1) * 512], start=(n == 0), stop=(n == SLOTS - 1))
                        last.then_inc(vused.sem, 2 if n == SLOTS - 1 else 1)
                    weave.upto(stage)
                weave.upto(END - 1)

            Weave(mixing(0, 1)).upto(END - 1)
            experts(0, FIRST, Weave(mixing(1, 2)))
            with pe.Fori(1, NB // 2 - 1) as b:
                experts(b, LOOP, Weave(mixing(b + 1, NB // 2)))
            with pe.Fori(NB // 2 - 1, NB - 1) as b:
                experts(b, LOOP, Weave(mixing(b + 1, NB)))
            experts(NB - 1, FINAL, Weave(iter(())))

        @block.vector
        def _(vec):
            ve = nc.vector
            setup = Steps(vec, bstep)
            steps = Steps(vec, vstep)
            pert = Steps(vec, pstep)
            ropes = Steps(vec, rstep)

            ve.memset(late_acc, 0.0).then_inc(s_lateclear, 1)
            vec.wait_ge(s_silu, 1)
            ve.tensor_copy(grid(mix, KC), over_last(scT, P)).then_inc(s_wide, 1)
            vec.wait_ge(s_consts, 2)
            vec.wait_ge(s_rows, 32)
            setup(ve.tensor_copy(iota16, iota_i))
            setup(ve.tensor_copy(pos_f, pos_i))
            setup(ve.tensor_tensor(grid(ang, NB), over_last(pos_f, HALF), over_first(inv_freq, NB), ALU.mult))
            RND = 12582912.0
            C1 = 6.28125
            C2 = float(2 * math.pi - 6.28125)
            PI = 3.1415925
            setup(ve.tensor_scalar(ang2, ang, 1.0 / (2 * math.pi), RND, ALU.mult, ALU.add))
            setup(ve.tensor_scalar(ang2, ang2, -RND, None, ALU.add))
            setup(ve.scalar_tensor_tensor(out=ang, in0=ang2, scalar=-C1, in1=ang, op0=ALU.mult, op1=ALU.add))
            setup(ve.scalar_tensor_tensor(out=ang, in0=ang2, scalar=-C2, in1=ang, op0=ALU.mult, op1=ALU.add))
            setup(ve.tensor_scalar(sinT, ang, PI, -PI, ALU.min, ALU.max))
            setup(ve.tensor_scalar(ang, ang, math.pi / 2, None, ALU.add))
            setup(ve.tensor_scalar(ang2, ang, math.pi, -2 * math.pi, ALU.is_gt, ALU.mult))
            setup(ve.tensor_tensor(ang, ang, ang2, ALU.add))
            ve.tensor_scalar(cosT, ang, PI, -PI, ALU.min, ALU.max).then_inc(s_ang, 1)
            vec.wait_ge(s_gain0, 16)
            vec.wait_ge(s_adaused, KC)
            ve.tensor_copy(B1, bank(0, 2))
            ve.scalar_tensor_tensor(out=A1, in0=bank(2, 2), scalar=1.0, in1=A1, op0=ALU.add, op1=ALU.mult)\
                .then_inc(s_mod, 1)
            vec.wait_ge(s_keyps, 1)
            ve.tensor_copy(keysT.rearrange("p a n -> p (a n)"), bank(4, 2)).then_inc(s_keysT, 1)
            vec.wait_ge(s_mod, 1)

            ve.memset(stag[:, 512:1024], 0.0)

            def modulate(b):
                a_root.wait(vec, b, 1)
                ropes(ve.reciprocal(rowsum, rowsum))
                ropes(ve.scalar_tensor_tensor(out=h2n, in0=x1n, scalar=rowsum, in1=A1,
                                              op0=ALU.mult, op1=ALU.mult))
                ve.tensor_tensor(h2n, h2n, B1, ALU.add).then_inc(a_h.sem, 1)

            def add_late(part):
                vec.wait_ge(s_laterow, 16 * (part + 1))
                for k in range(KC):
                    n = part * KC + k
                    vec.wait_ge(s_ada[n % 2], 16 * (2 + n // 2 + 1))
                    ve.scalar_tensor_tensor(out=late_acc, in0=late_buf[n % 2], scalar=scT[:, k:k + 1], in1=late_acc,
                                            op0=ALU.mult, op1=ALU.add).then_inc(s_lateused, 1)
                    vec.wait_ge(s_lateused, n + 1)

            def take_late(part):
                vec.wait_ge(s_latepsum, part + 1)
                vec.wait_ge(s_gain, 16 * 4)
                what = LATE_PARTS[part]
                if what == SH2:
                    ve.tensor_copy(B2, VB).then_inc(s_mod, 1)
                elif what == SC2:
                    ve.scalar_tensor_tensor(out=A2, in0=VB, scalar=1.0, in1=A2, op0=ALU.add, op1=ALU.mult)\
                        .then_inc(s_mod, 1)
                else:
                    dst = P1 if what == G1 else P2
                    ve.tensor_tensor(dst, VB, dst, ALU.mult).then_inc(s_mod, 1)
                if part < len(LATE_PARTS) - 1:
                    ve.memset(late_acc, 0.0).then_inc(s_lateclear, 1)

            def project(b, more):
                late = LATE_IN.get(b) if isinstance(b, int) else None
                if more:
                    modulate(b + 1)
                if late is not None:
                    add_late(late)
                a_raw.wait(vec, b, 1)
                a_rps.wait(vec, b, 0)
                heads = 14 if few_keys(b) else 22
                r3, o3 = (grid(tile[:, 0:heads * HD], heads) for tile in (raw, rot))
                t3 = grid(rtmp[:, 0:heads * HALF], heads)
                cos = over_first(grid(cosT, NB)[:, b, :], heads)
                sin = over_first(grid(sinT, NB)[:, b, :], heads)
                x1, x2 = r3[:, :, 0:HALF], r3[:, :, HALF:HD]
                ropes(ve.tensor_tensor(t3, x2, sin, ALU.mult))
                ropes(ve.tensor_tensor(o3[:, :, 0:HALF], x1, cos, ALU.mult))
                ropes(ve.tensor_tensor(o3[:, :, 0:HALF], o3[:, :, 0:HALF], t3, ALU.subtract))
                ropes(ve.tensor_tensor(t3, x1, sin, ALU.mult))
                ropes(ve.tensor_tensor(o3[:, :, HALF:HD], x2, cos, ALU.mult))
                ve.tensor_tensor(o3[:, :, HALF:HD], o3[:, :, HALF:HD], t3, ALU.add).then_inc(a_rope.sem, 1)
                if late is not None:
                    take_late(late)
                a_proj.wait(vec, b, 6)
                a_out.wait(vec, b, 0)
                ve.tensor_copy(stag[:, 1536:2560], bank(6, 2)).then_inc(a_xbc.sem, 1)

            ropes.begin()
            modulate(0)
            vec.wait_ge(s_trig, 1)
            for b in range(4):
                if b:
                    ropes.begin()
                project(b, True)
            with vec.Fori(4, NB - 1) as b:
                ropes.begin()
                project(b, True)
            ropes.begin()
            project(NB - 1, False)

            def mixing(b, nb):
                steps.begin()
                yield 0
                m_xbc.wait(vec, b, 16)
                steps(ve.tensor_copy(xc[:, :, 0:3], hist))
                w3 = grid(convw, TAPS)
                steps(ve.tensor_tensor(cv, xc[:, :, 3:131], over_last(w3[:, 3, :], P), ALU.mult))
                for j in range(3):
                    yield 2 + 2 * j
                    steps(ve.tensor_tensor(ctmp, xc[:, :, j:j + P], over_last(w3[:, j, :], P),
                                           ALU.mult))
                    yield 3 + 2 * j
                    if j < 2:
                        steps(ve.tensor_tensor(cv, cv, ctmp, ALU.add))
                    else:
                        ve.tensor_tensor(cv, cv, ctmp, ALU.add).then_inc(conv.sem, 1)
                steps(ve.tensor_copy(hist, xc[:, :, 128:131]))
                adt_b, dt_b = grid(adt, NB)[:, b, :], grid(dt_s, NB)[:, b, :]
                yield 9
                ve.tensor_tensor(gh, over_first(after, 4), over_last(adt_b[:, 0:4], P), ALU.mult)\
                    .then_inc(ghr.sem, 1)
                yield 13
                chanT.wait(vec, b, 2)
                steps(ve.tensor_copy(xtok, XB))
                steps(ve.tensor_tensor(grid(xdt, HEADS), grid(XB, HEADS), over_last(dt_b, HD), ALU.mult))
                ve.tensor_copy(btok, OB[:, 0:256]).then_inc(tok.sem, 1)
                yield 15
                ve.tensor_tensor(grid(xw, HEADS), grid(xdt, HEADS), over_last(grid(dec, NB)[:, b, :], HD),
                                 ALU.mult).then_inc(xwr.sem, 1)
                cbps.wait(vec, b, 1)
                steps(ve.tensor_tensor(cbm, bank(4)[:, 0:256].rearrange("p (g n) -> p g n", g=2),
                                       over_first(upto, 2), ALU.mult))
                yield 17
                seg.wait(vec, b, 1)
                ve.tensor_tensor(gh, over_first(after, 4), over_last(adt_b[:, 4:8], P), ALU.mult)\
                    .then_inc(ghr.sem, 1)
                for g in range(2):
                    yield 19 + 2 * g
                    decay.wait(vec, b, g + 1)
                    lg = grid(L[:, g * 512:(g + 1) * 512], 4)
                    ve.tensor_tensor(lg, lg, over_first(cbm[:, g, :], 4), ALU.mult).then_inc(masked.sem, 1)
                yield 23
                yoff.wait(vec, b, 1)
                steps(ve.tensor_tensor(grid(yy, HEADS), grid(OB, HEADS), over_last(grid(eac, NB)[:, b, :], HD),
                                       ALU.mult))
                steps(ve.tensor_tensor(grid(state, HEADS), grid(state, HEADS),
                                       over_last(grid(etot, NB)[:, b, :], HD), ALU.mult))
                stps.wait(vec, b, 1)
                ve.tensor_tensor(state, state, XB, ALU.add).then_inc(stdone.sem, 1)
                yield 25
                ydiag.wait(vec, b, 1)
                steps(ve.tensor_tensor(yy, yy, bank(5), ALU.add))
                steps(ve.tensor_tensor(grid(ytmp, HEADS), grid(xtok, HEADS), over_last(dskip, HD), ALU.mult))
                steps(ve.tensor_tensor(yy, yy, ytmp, ALU.add))
                zgate.wait(vec, b, 1)
                ve.tensor_tensor(yy, yy, zt, ALU.mult).then_inc(gated.sem, 1)
                yield 28
                ssdrms.wait(vec, b, 1)
                steps(ve.reciprocal(stat[:, 0:1], stat[:, 0:1]))
                ve.scalar_tensor_tensor(out=mix[:, 512:1024], in0=yy, scalar=stat[:, 0:1], in1=ssdg,
                                        op0=ALU.mult, op1=ALU.mult).then_inc(ssdout.sem, 1)
                wb = grid(wis, NB)[:, b, :]
                nk = nb * P
                scores, unseen = SC[:, 0:nk], AM[:, 0:nk]
                if nb > SHORT:
                    for h in range(HEADS):
                        yield 30 + h
                        relu.wait(vec, b, h + 1)
                        if h == 0:
                            ve.tensor_scalar(scores, RL[0][:, 0:nk], wb[:, 0:1], None, ALU.mult)\
                                .then_inc(scacc.sem, 1)
                        else:
                            scacc.wait(vec, b, h)
                            ve.scalar_tensor_tensor(out=scores, in0=RL[h % 2][:, 0:nk], scalar=wb[:, h:h + 1],
                                                    in1=scores, op0=ALU.mult, op1=ALU.add).then_inc(scacc.sem, 1)
                    yield 38
                    scacc.wait(vec, b, HEADS)
                    vec.sem_inc(s_turn, 1)
                    mask = causal[:, bass.ds((NB - 1 - b) * P, nk)]
                    steps(ve.tensor_tensor(scores, scores, mask, ALU.add))
                    for i in range(TOPK // 8):
                        yield 39 + i * 74 / 32
                        if i:
                            steps.after(replaced)
                        found = steps.count(ve.max(mx8, scores))
                        yield 40 + i * 74 / 32
                        steps.after(found)
                        replaced = steps.count(ve.match_replace(scores, mx8, scores, TAKEN))
                    yield 113
                    steps.after(replaced)
                    steps(ve.tensor_scalar(unseen, scores, LOW, NEG, ALU.is_gt, ALU.mult))
                    yield 115
                    steps(ve.tensor_tensor(unseen, unseen, mask, ALU.add))
                else:
                    steps(ve.tensor_copy(unseen, causal[:, (NB - 1 - b) * P:(NB - 1 - b) * P + nk]))
                for h in range(HEADS):
                    yield 116 + 3 * h
                    sps.wait(vec, b, h + 1)
                    if h >= 2:
                        ptps.wait(vec, b, h - 1)
                    ve.scalar_tensor_tensor(out=RL[h % 2][:, 0:nk], in0=SB[:, 0:nk], scalar=HD ** -0.5, in1=unseen,
                                            op0=ALU.mult, op1=ALU.add).then_inc(sread.sem, 1)
                    yield 117 + 3 * h
                    sread.wait(vec, b, h + 1)
                    ve.tensor_reduce(negmax[:, h:h + 1], RL[h % 2][:, 0:nk], AX.X, ALU.max, negate=True)\
                        .then_inc(smax.sem, 1)
                yield 143
                av.wait(vec, b, HEADS)
                steps(ve.reciprocal(rsums, psums))
                ve.tensor_tensor(grid(mix[:, 0:512], HEADS), grid(OB, HEADS), over_last(rsums, HD), ALU.mult)\
                    .then_inc(mixr.sem, 1)
                yield 149
                outrms.wait(vec, b, 1)
                m_x.wait(vec, b, 16)
                steps(ve.reciprocal(stat[:, 1:2], stat[:, 1:2]))
                steps(ve.scalar_tensor_tensor(out=otmp, in0=SB, scalar=stat[:, 1:2], in1=P1,
                                              op0=ALU.mult, op1=ALU.mult))
                yield 150
                ve.tensor_tensor(x1n, x1n, otmp, ALU.add).then_inc(x1r.sem, 1)
                yield 152
                x1rms.wait(vec, b, 1)
                steps(ve.reciprocal(stat[:, 2:3], stat[:, 2:3]))
                steps(ve.scalar_tensor_tensor(out=h2n, in0=x1n, scalar=stat[:, 2:3], in1=A2,
                                              op0=ALU.mult, op1=ALU.mult))
                yield 154
                ve.tensor_tensor(h2n, h2n, B2, ALU.add).then_inc(h2r.sem, 1)
                def top16(values, places, s, i, width):
                    s = s[:, i * width:(i + 1) * width]
                    lo, hi = slice(i * PK, i * PK + 8), slice(i * PK + 8, (i + 1) * PK)
                    yield ve.max(values[:, lo], s)
                    yield ve.max_index(places[:, lo], values[:, lo], s)
                    yield ve.match_replace(s, values[:, lo], s, TAKEN)
                    yield ve.max(values[:, hi], s)
                    yield ve.max_index(places[:, hi], values[:, hi], s)

                def two_lists(values, places, s, i, width):
                    lists = [top16(values, places, s, i + j, width) for j in range(2)]
                    before = [None, None]
                    for _ in range(5):
                        for j in range(2):
                            if before[j]:
                                steps.after(before[j])
                            before[j] = steps.count(next(lists[j]))

                for i in range(0, LISTS, 2):
                    yield 162 + i
                    if i % 8 == 0:
                        s2.wait(vec, b, i // 8 + 1)
                        vec.sem_inc(s_turn, 1)
                    two_lists(sv, si, ss, i, P)
                yield 178
                steps.after(steps.n)
                steps(ve.tensor_copy(sif, si))
                sv4 = sv.rearrange("p (t h k) -> p t h k", h=HEADS, t=2)
                cand4 = cand.rearrange("p (h i j) -> p h i j", h=HEADS, i=PK)
                for h in range(HEADS):
                    summed = steps.count(ve.tensor_tensor(cand4[:, h], over_last(sv4[:, 0, h], PK),
                                                          over_first(sv4[:, 1, h], PK), ALU.add))
                steps.after(summed)
                for h in range(0, HEADS, 2):
                    yield 181 + 2 * h
                    two_lists(fv, fp, cand, h, PK * PK)
                steps.after(steps.n)
                yield 195
                steps(ve.tensor_reduce(gsum, grid(fv, HEADS), AX.X, ALU.max))
                ve.tensor_tensor(grid(gn, HEADS), grid(fv, HEADS), over_last(gsum, PK), ALU.subtract)\
                    .then_inc(fvr.sem, 1)
                idxc.wait(vec, b, 0)
                hot3 = hot.rearrange("p (n k) -> p n k", k=PK)
                for t in range(2):
                    yield 197 + 4 * t
                    if t == 0:
                        steps(ve.tensor_scalar(fpi, fp, 4, None, ALU.logical_shift_right))
                    else:
                        steps(ve.tensor_scalar(fpi, fp, 15, None, ALU.bitwise_and))
                    steps(ve.tensor_copy(fpf, fpi))
                    steps(ve.tensor_tensor(hot3, over_first(iota16, SLOTS), over_last(fpf, PK), ALU.is_equal))
                    yield 199 + 4 * t
                    sif4 = sif.rearrange("p (t h k) -> p t h k", h=HEADS, t=2)
                    for h in range(HEADS):
                        hh = hot3[:, h * PK:(h + 1) * PK, :]
                        picked = steps.count(ve.tensor_tensor(hh, hh, over_first(sif4[:, t, h], PK), ALU.mult))
                    steps.after(picked)
                    steps(ve.tensor_reduce((e1, e2)[t], hot3, AX.X, ALU.add))
                steps(ve.scalar_tensor_tensor(out=e1, in0=e1, scalar=float(EXPERT_KEYS), in1=e2,
                                              op0=ALU.mult, op1=ALU.add))
                steps(ve.tensor_copy(idxn, e1))
                gexp.wait(vec, b, 1)
                steps(ve.tensor_reduce(gsum, grid(gn, HEADS), AX.X, ALU.add))
                steps(ve.reciprocal(gsum, gsum))
                ve.tensor_tensor(grid(gn, HEADS), grid(gn, HEADS), over_last(gsum, PK), ALU.mult)\
                    .then_inc(prep.sem, 1)

            def finish(b, back):
                xcommit.wait(vec, b, 1 - back)
                frms.wait(vec, b, 1 - back)
                pert(ve.reciprocal(stat[:, 3:4], stat[:, 3:4]))
                pert(ve.scalar_tensor_tensor(out=VB, in0=VB, scalar=stat[:, 3:4], in1=P2,
                                             op0=ALU.mult, op1=ALU.mult))
                ve.tensor_tensor(x1c, x1c, VB, ALU.add).then_inc(xfin.sem, 1)

            def experts(b, plan_steps, weave):
                at = moments(plan_steps)
                pert.begin()
                prep.wait(vec, b, 1)
                dot.wait(vec, b, 0)
                wready.wait(vec, b, 0)
                ve.tensor_copy(gc, gn)
                pert(ve.tensor_copy(h2c, h2n))
                for i in range(max(max(at) + 1, len(plan_steps))):
                    for what, h in at.get(i, ()):
                        if what == "weights":
                            s = slice(h * PK, (h + 1) * PK)
                            gelu.wait(vec, b, h + 1)
                            if plan_steps is not FIRST:
                                dg.wait(vec, b, (h + 1) * PK - SLOTS)
                            ve.tensor_tensor(wgt[:, s], gel[:, s], gc[:, s], ALU.mult).then_inc(wready.sem, 1)
                        if what == "finish" and plan_steps is not FIRST:
                            finish(b, 1)
                        if what == "commit":
                            xout.wait(vec, b, 0)
                            ve.tensor_copy(x1c, x1n).then_inc(xcommit.sem, 1)
                    if i >= len(plan_steps):
                        continue
                    kind, n, stage = plan_steps[i]
                    if kind == "u":
                        r = n % UR
                        vec.wait_ge(u_in[r], 16 * (b * uses(UR, r) + n // UR + 1))
                        ve.tensor_tensor_reduce(u_ring[r], u_ring[r], h2c, 1.0, 0.0, ALU.mult, ALU.add,
                                                dots[:, n:n + 1]).then_inc(dot.sem, 1)
                    weave.upto(stage)
                weave.upto(END - 1)

            first = Weave(mixing(0, 1))
            small3 = [small[:, i * 64:(i + 1) * 64] for i in range(6)]
            a_rot.wait(vec, NB, 0)
            vec.wait_ge(s_small, 16 * 5)
            vec.wait_ge(s_mod, 5)
            dw = grid(dtwi, NB)
            setup(ve.tensor_scalar(grid(wis, NB), dw[:, :, 0:8], float(HEADS ** -0.5), None, ALU.mult))
            setup(ve.tensor_tensor(grid(small3[2], NB), dw[:, :, 8:16], over_first(dtb, NB), ALU.add))
            setup(ve.tensor_scalar(small3[3], small3[2], 0.0, None, ALU.max))
            setup(ve.tensor_scalar(small3[4], small3[2], -1.0, None, ALU.mult))
            ve.tensor_tensor(small3[0], small3[2], small3[4], ALU.max).then_inc(s_dtv, 1)
            first.upto(1)
            vec.wait_ge(s_dta, 1)
            setup(ve.tensor_scalar(neg_a, neg_a, -1.0, None, ALU.mult))
            setup(ve.tensor_scalar(small3[1], small3[0], 1.0, None, ALU.add))
            setup(ve.tensor_scalar(small3[2], small3[1], -1.0, None, ALU.add))
            setup(ve.tensor_scalar(small3[4], small3[2], 1e-30, None, ALU.max))
            setup(ve.reciprocal(small3[4], small3[4]))
            ve.tensor_tensor(small3[4], small3[4], small3[0], ALU.mult).then_inc(s_dtv, 1)
            first.upto(3)
            vec.wait_ge(s_dta, 2)
            setup(ve.tensor_tensor(small3[4], small3[4], small3[1], ALU.mult))
            setup(ve.scalar_tensor_tensor(out=small3[5], in0=small3[2], scalar=0.0, in1=small3[0],
                                          op0=ALU.is_equal, op1=ALU.mult))
            setup(ve.tensor_tensor(small3[4], small3[4], small3[5], ALU.add))
            setup(ve.tensor_tensor(dt_s, small3[4], small3[3], ALU.add))
            ve.tensor_tensor(grid(adt, NB), grid(dt_s, NB), over_first(neg_a, NB), ALU.mult).then_inc(s_dtv, 1)
            first.upto(5)
            vec.wait_ge(s_dtp, 1)
            setup(ve.tensor_copy(small3[0], XB[:, 64:128]))
            ve.tensor_tensor(small3[0], small3[0], XB[:, 0:64], ALU.subtract).then_inc(s_dtv, 1)
            vec.wait_ge(s_dta, 3)

            first.upto(END - 1)
            experts(0, FIRST, Weave(mixing(1, 2)))
            with vec.Fori(1, NB // 2 - 1) as b:
                experts(b, LOOP, Weave(mixing(b + 1, NB // 2)))
            with vec.Fori(NB // 2 - 1, NB - 1) as b:
                experts(b, LOOP, Weave(mixing(b + 1, NB)))
            experts(NB - 1, FINAL, Weave(iter(())))
            finish(NB - 1, 0)


_INS = ['x', 'c', 'positions', 'w_ada', 'b_ada', 'pre_mix_g', 'post_mix_g', 'w_in', 'conv_w', 'conv_b', 'dt_bias',
        'a_log', 'd_skip', 'ssd_norm_g', 'w_out', 'pre_ffn_g', 'post_ffn_g', 'peer_w_q', 'peer_sub_keys',
        'peer_u', 'peer_v']


def kernel(**inputs):
    import numpy as _np
    import concourse.bacc as _bacc
    from concourse import mybir as _mybir
    from concourse.bass_utils import run_bass_kernel_spmd as _run

    nc = _bacc.Bacc("TRN2", target_bir_lowering=False, num_devices=1)
    arrays, args = {}, []
    for name in _INS:
        a = _np.ascontiguousarray(inputs[name])
        arrays[f"in_{name}"] = a
        args.append(nc.dram_tensor(f"in_{name}", a.shape, _mybir.dt.from_np(a.dtype), kind="ExternalInput").ap())
    res = nc.dram_tensor("out_x", (1, SEQ, D), F32, kind="ExternalOutput").ap()
    hybrid_block(nc, *args, res)
    r = _run(nc, [arrays], core_ids=[0])
    return r.results[0]["out_x"]
```
